# Optimizing a Trainium2 kernel written in Bass

```python
import jax, jax.numpy as jnp
from jax import lax
import numpy as np

D_MODEL = 1024
BATCH = 1
SEQ = 256
DEPTH = 1
DEC_BATCH = 1
DEC_SEQ = 64
PAST_LEN = 128

CHUNK = 64
LEFT_CHUNKS = 8
ATT_WINDOW = LEFT_CHUNKS * CHUNK
BAND = ATT_WINDOW + CHUNK
N_HEADS = 16
HEAD_DIM = 64
D_ATT = N_HEADS * HEAD_DIM
MAX_REL = 128
N_REL = 2 * MAX_REL + 1
D_CONV = D_MODEL
CONV_WIDTH = 31
N_EXPERTS = 32
TOP_K = 4
D_EXPERT = D_MODEL
SWIGLU_LIMIT = 7.0
SWIGLU_ALPHA = 1.702
MOE_BLOCK = 128
LN_EPS = 1e-5
NEG_INF = -1e30
DN_ALPHA = (2 * DEPTH) ** 0.25
DN_BETA = (8 * DEPTH) ** -0.25
C_IN = 3 * D_ATT + 2 * D_CONV + 2 * D_MODEL
SPLITS = (D_ATT, 2 * D_ATT, 3 * D_ATT, 3 * D_ATT + D_CONV, 3 * D_ATT + 2 * D_CONV,
          3 * D_ATT + 2 * D_CONV + D_MODEL)

kernel_name = 'streaming_band_attn_conformer_conv_moe'

def layer_norm(x, g, b):
    xf = x.astype(jnp.float32)
    mu = xf.mean(-1, keepdims=True)
    var = jnp.square(xf - mu).mean(-1, keepdims=True)
    return ((xf - mu) * lax.rsqrt(var + LN_EPS)).astype(x.dtype) * g + b

def split_in_proj(x, w, b):
    h = x @ w + b
    q, k, v, ua, ub, ga, gb = jnp.split(h, SPLITS, axis=-1)
    hs = x.shape[:-1] + (N_HEADS, HEAD_DIM)
    u = ua * jax.nn.sigmoid(ub)
    return q.reshape(hs), k.reshape(hs), v.reshape(hs), u, ga, gb

def band_attention(q, k, v, q_pos, k_pos, rel_bias):
    s = jnp.einsum('bqhd,bkhd->bhqk', q, k).astype(jnp.float32) * (HEAD_DIM ** -0.5)
    rel = jnp.clip(q_pos[:, None] - k_pos[None, :], -MAX_REL, MAX_REL) + MAX_REL
    s = s + rel_bias[:, rel].astype(jnp.float32)[None]
    q_chunk = q_pos[:, None] // CHUNK
    k_chunk = k_pos[None, :] // CHUNK
    allowed = (k_pos[None, :] >= 0) & (k_chunk <= q_chunk) & (k_chunk >= q_chunk - LEFT_CHUNKS)
    s = jnp.where(allowed[None, None], s, NEG_INF)
    p = jax.nn.softmax(s, axis=-1).astype(v.dtype)
    return jnp.einsum('bhqk,bkhd->bqhd', p, v)

def conv_branch(u_ext, w_dw, b_dw, g, b, w_pw):
    y = lax.conv_general_dilated(u_ext, w_dw[:, None, :], window_strides=(1,), padding='VALID',
                                 dimension_numbers=('NWC', 'WIO', 'NWC'),
                                 feature_group_count=D_CONV) + b_dw
    y = layer_norm(y, g, b)
    return jax.nn.silu(y) @ w_pw

def moe(x, w_router, b_router, w_gate, b_gate, w_up, b_up, w_down, b_down):
    n, d = x.shape
    logits = (x @ w_router + b_router).astype(jnp.float32)
    top_val, top_idx = lax.top_k(logits, TOP_K)
    gate = jax.nn.softmax(top_val, axis=-1).astype(x.dtype)
    nk = n * TOP_K
    n_blocks = -(-nk // MOE_BLOCK) + N_EXPERTS
    flat_e = top_idx.reshape(-1)
    flat_tok = jnp.arange(nk, dtype=jnp.int32) // TOP_K
    order = jnp.argsort(flat_e, stable=True)
    sorted_e = flat_e[order]
    counts = jnp.zeros((N_EXPERTS,), jnp.int32).at[flat_e].add(1)
    start = jnp.cumsum(counts) - counts
    padded = (counts + MOE_BLOCK - 1) // MOE_BLOCK * MOE_BLOCK
    pad_end = jnp.cumsum(padded)
    pad_start = pad_end - padded
    dest = pad_start[sorted_e] + jnp.arange(nk, dtype=jnp.int32) - start[sorted_e]
    sorted_tok = flat_tok[order]
    row_tok = jnp.full((n_blocks * MOE_BLOCK,), n, jnp.int32).at[dest].set(sorted_tok)
    block_e = jnp.minimum(jnp.searchsorted(pad_end, jnp.arange(n_blocks, dtype=jnp.int32) * MOE_BLOCK,
                                           side='right'), N_EXPERTS - 1).astype(jnp.int32)
    x_pad = jnp.concatenate([x, jnp.zeros((1, d), x.dtype)], axis=0)
    xb = x_pad[row_tok].reshape(n_blocks, MOE_BLOCK, d)

    def expert_block(args):
        xe, e = args
        gt = jnp.minimum(xe @ w_gate[e] + b_gate[e], SWIGLU_LIMIT)
        up = jnp.clip(xe @ w_up[e] + b_up[e], -SWIGLU_LIMIT, SWIGLU_LIMIT)
        h = gt * jax.nn.sigmoid(SWIGLU_ALPHA * gt) * (up + 1.0)
        return h @ w_down[e] + b_down[e]

    yb = lax.map(expert_block, (xb, block_e)).reshape(n_blocks * MOE_BLOCK, d)
    y_assign = yb[dest] * gate.reshape(-1)[order][:, None]
    return jnp.zeros_like(x).at[sorted_tok].add(y_assign)

def setup_inputs(seed: int = 0) -> dict:
    key = jax.random.key(seed)
    ks = jax.random.split(key, 32)
    f32 = jnp.float32

    def nrm(k, shape, scale):
        return jax.random.normal(k, shape, f32) * scale

    att_cache = min(ATT_WINDOW, PAST_LEN)
    w_in = nrm(ks[5], (DEPTH, D_MODEL, C_IN), D_MODEL ** -0.5)
    w_in = w_in.at[:, :, 2 * D_ATT:3 * D_ATT].multiply(DN_BETA)
    return {
        'x_prompt': nrm(ks[0], (BATCH, SEQ, D_MODEL), 1.0),
        'x_sample': nrm(ks[1], (DEC_BATCH, DEC_SEQ, D_MODEL), 1.0),
        'cache_k': nrm(ks[2], (DEPTH, DEC_BATCH, att_cache, N_HEADS, HEAD_DIM), 1.0),
        'cache_v': nrm(ks[3], (DEPTH, DEC_BATCH, att_cache, N_HEADS, HEAD_DIM), 0.5),
        'state_conv': nrm(ks[4], (DEPTH, DEC_BATCH, CONV_WIDTH - 1, D_CONV), 0.5),
        'w_in': w_in,
        'b_in': nrm(ks[6], (DEPTH, C_IN), 0.02),
        'rel_bias': nrm(ks[7], (DEPTH, N_HEADS, N_REL), 0.1),
        'w_att_o': nrm(ks[8], (DEPTH, D_ATT, D_MODEL), D_ATT ** -0.5 * DN_BETA),
        'w_dw': nrm(ks[9], (DEPTH, CONV_WIDTH, D_CONV), CONV_WIDTH ** -0.5),
        'b_dw': nrm(ks[10], (DEPTH, D_CONV), 0.02),
        'conv_ln_g': 1.0 + nrm(ks[11], (DEPTH, D_CONV), 0.02),
        'conv_ln_b': nrm(ks[12], (DEPTH, D_CONV), 0.02),
        'w_pw': nrm(ks[13], (DEPTH, D_CONV, D_MODEL), D_CONV ** -0.5 * DN_BETA),
        'w_out': nrm(ks[14], (DEPTH, D_MODEL, D_MODEL), D_MODEL ** -0.5 * DN_BETA),
        'b_out': nrm(ks[15], (DEPTH, D_MODEL), 0.02),
        'ln1_g': 1.0 + nrm(ks[16], (DEPTH, D_MODEL), 0.02),
        'ln1_b': nrm(ks[17], (DEPTH, D_MODEL), 0.02),
        'w_router': nrm(ks[18], (DEPTH, D_MODEL, N_EXPERTS), D_MODEL ** -0.5),
        'b_router': nrm(ks[19], (DEPTH, N_EXPERTS), 0.01),
        'w_gate': nrm(ks[20], (DEPTH, N_EXPERTS, D_MODEL, D_EXPERT), D_MODEL ** -0.5 * DN_BETA),
        'b_gate': nrm(ks[21], (DEPTH, N_EXPERTS, D_EXPERT), 0.02),
        'w_up': nrm(ks[22], (DEPTH, N_EXPERTS, D_MODEL, D_EXPERT), D_MODEL ** -0.5 * DN_BETA),
        'b_up': nrm(ks[23], (DEPTH, N_EXPERTS, D_EXPERT), 0.02),
        'w_down': nrm(ks[24], (DEPTH, N_EXPERTS, D_EXPERT, D_MODEL), D_EXPERT ** -0.5 * DN_BETA),
        'b_down': nrm(ks[25], (DEPTH, N_EXPERTS, D_MODEL), 0.02),
        'ln2_g': 1.0 + nrm(ks[26], (DEPTH, D_MODEL), 0.02),
        'ln2_b': nrm(ks[27], (DEPTH, D_MODEL), 0.02),
    }

def reference(x_prompt, x_sample, cache_k, cache_v, state_conv, w_in, b_in, rel_bias, w_att_o,
              w_dw, b_dw, conv_ln_g, conv_ln_b, w_pw, w_out, b_out, ln1_g, ln1_b, w_router,
              b_router, w_gate, b_gate, w_up, b_up, w_down, b_down, ln2_g, ln2_b):
    B, S, _ = x_prompt.shape
    Bd, T, _ = x_sample.shape
    W = cache_k.shape[2]
    n_chunks = S // CHUNK
    keep_p = min(ATT_WINDOW, S)
    q_pos_s = PAST_LEN + jnp.arange(T, dtype=jnp.int32)
    k_pos_s = PAST_LEN - W + jnp.arange(W + T, dtype=jnp.int32)

    xp, xs = x_prompt, x_sample
    nkp, nvp, ncp, nks, nvs, ncs = [], [], [], [], [], []
    for l in range(DEPTH):
        rb = rel_bias[l]
        q, k, v, u, ga, gb = split_in_proj(xp, w_in[l], b_in[l])
        zpad = jnp.zeros((B, ATT_WINDOW, N_HEADS, HEAD_DIM), k.dtype)
        k_ext = jnp.concatenate([zpad, k], axis=1)
        v_ext = jnp.concatenate([zpad, v], axis=1)

        def chunk_attn(c):
            start = c * CHUNK
            qc = lax.dynamic_slice_in_dim(q, start, CHUNK, axis=1)
            kc = lax.dynamic_slice_in_dim(k_ext, start, BAND, axis=1)
            vc = lax.dynamic_slice_in_dim(v_ext, start, BAND, axis=1)
            q_pos = start + jnp.arange(CHUNK, dtype=jnp.int32)
            k_pos = start - ATT_WINDOW + jnp.arange(BAND, dtype=jnp.int32)
            return band_attention(qc, kc, vc, q_pos, k_pos, rb)

        o = lax.map(chunk_attn, jnp.arange(n_chunks, dtype=jnp.int32))
        y_att = jnp.moveaxis(o, 0, 1).reshape(B, S, D_ATT) @ w_att_o[l]
        u_ext = jnp.concatenate([jnp.zeros((B, CONV_WIDTH - 1, D_CONV), u.dtype), u], axis=1)
        y_conv = conv_branch(u_ext, w_dw[l], b_dw[l], conv_ln_g[l], conv_ln_b[l], w_pw[l])
        mix = jax.nn.sigmoid(ga) * y_att + jax.nn.sigmoid(gb) * y_conv
        xp = layer_norm(DN_ALPHA * xp + mix @ w_out[l] + b_out[l], ln1_g[l], ln1_b[l])
        ff = moe(xp.reshape(B * S, D_MODEL), w_router[l], b_router[l], w_gate[l], b_gate[l],
                 w_up[l], b_up[l], w_down[l], b_down[l]).reshape(B, S, D_MODEL)
        xp = layer_norm(DN_ALPHA * xp + ff, ln2_g[l], ln2_b[l])
        nkp.append(k[:, S - keep_p:])
        nvp.append(v[:, S - keep_p:])
        ncp.append(u_ext[:, S:])

        q, k, v, u, ga, gb = split_in_proj(xs, w_in[l], b_in[l])
        k_ext = jnp.concatenate([cache_k[l], k], axis=1)
        v_ext = jnp.concatenate([cache_v[l], v], axis=1)
        o = band_attention(q, k_ext, v_ext, q_pos_s, k_pos_s, rb)
        y_att = o.reshape(Bd, T, D_ATT) @ w_att_o[l]
        u_ext = jnp.concatenate([state_conv[l], u], axis=1)
        y_conv = conv_branch(u_ext, w_dw[l], b_dw[l], conv_ln_g[l], conv_ln_b[l], w_pw[l])
        mix = jax.nn.sigmoid(ga) * y_att + jax.nn.sigmoid(gb) * y_conv
        xs = layer_norm(DN_ALPHA * xs + mix @ w_out[l] + b_out[l], ln1_g[l], ln1_b[l])
        ff = moe(xs.reshape(Bd * T, D_MODEL), w_router[l], b_router[l], w_gate[l], b_gate[l],
                 w_up[l], b_up[l], w_down[l], b_down[l]).reshape(Bd, T, D_MODEL)
        xs = layer_norm(DN_ALPHA * xs + ff, ln2_g[l], ln2_b[l])
        nks.append(k_ext[:, T:])
        nvs.append(v_ext[:, T:])
        ncs.append(u_ext[:, T:])

    y_prompt = xp
    y_sample = xs
    new_k_prompt = jnp.stack(nkp, axis=0)
    new_v_prompt = jnp.stack(nvp, axis=0)
    new_conv_prompt = jnp.stack(ncp, axis=0)
    new_k_sample = jnp.stack(nks, axis=0)
    new_v_sample = jnp.stack(nvs, axis=0)
    new_conv_sample = jnp.stack(ncs, axis=0)
    return (y_prompt, y_sample, new_k_prompt, new_v_prompt, new_conv_prompt,
            new_k_sample, new_v_sample, new_conv_sample)


_drawn_inputs = setup_inputs


def setup_inputs(seed=0):
    import zlib

    import numpy as np

    out = dict(_drawn_inputs(seed))
    spreads = {}
    factors = {'rel_bias': 33.156,
     'w_att_o': 3.248,
     'b_dw': 8.0,
     'conv_ln_g': 26.74,
     'conv_ln_b': 26.521,
     'b_out': 9.145,
     'b_router': 6.077,
     'b_gate': 8.0,
     'b_up': 28.302,
     'b_down': 6.257,
     'ln2_g': 21.938,
     'ln2_b': 24.299}
    for name, (base, spread) in spreads.items():
        noise = np.random.default_rng([zlib.crc32(name.encode()), seed]).standard_normal(out[name].shape)
        drawn = base * np.exp(spread * noise) if base else spread * noise
        out[name] = __import__('jax').numpy.asarray(drawn.astype(out[name].dtype))
    for name, factor in factors.items():
        out[name] = (out[name] * factor).astype(out[name].dtype)
    return out
```

```python
from contextlib import ExitStack

import concourse.bass as bass
from concourse import mybir

ALU = mybir.AluOpType
ACT = mybir.ActivationFunctionType
AXX = mybir.AxisListType.X
F32 = mybir.dt.float32
BF16 = mybir.dt.bfloat16
F16 = mybir.dt.float16
I32 = mybir.dt.int32
U32 = mybir.dt.uint32

P = 128
D = 1024
KC = D // P
NP_, NS_ = 256, 64
T = NP_ + NS_
TT = [(0, 128), (128, 128), (256, 64)]
H, HD = 16, 64
PAIRS = H // 2
PAST = 128
KW = 31
HALO = KW - 1
UEXT = 384
US = HALO + NP_ + HALO
CONVN = NP_ + HALO + NS_
E = 32
TOPK = 4
SLOTS = 64
SMALL = 32
MAXREL = 128
NREL = 2 * MAXREL + 1
REV = 384
ALPHA = 2.0 ** 0.25
EPS = 1e-5
LIMIT = 7.0
SW_ALPHA = 1.702
SCALE = HD ** -0.5
NEG = -1e30


def encoder_step(nc, x_prompt, x_sample, cache_k, cache_v, state_conv, w_in, b_in, rel_bias, w_att_o,
                 w_dw, b_dw, conv_ln_g, conv_ln_b, w_pw, w_out, b_out, ln1_g, ln1_b, w_router, b_router,
                 w_gate, b_gate, w_up, b_up, w_down, b_down, ln2_g, ln2_b,
                 y_prompt, y_sample, new_k_p, new_v_p, new_conv_p, new_k_s, new_v_s, new_conv_s):
    BROW = H * REV
    rev_dram = nc.dram_tensor("rev_bias", [P, BROW + 1], F32, kind="Internal").ap()

    def rows(ap):
        return ap[0].rearrange("(c p) n -> p c n", p=P)

    w_in_v = rows(w_in).rearrange("p c (b s n) -> p c b s n", s=2, n=512)
    w_pw_v, w_att_v, w_out_v = (rows(w).rearrange("p c (s n) -> p c s n", s=2) for w in (w_pw, w_att_o, w_out))
    wg_v, wu_v, wd_v = (w[0].rearrange("e (c p) n -> e p c n", p=P) for w in (w_gate, w_up, w_down))
    ck_v = cache_k[0, 0].rearrange("t h d -> t (h d)")
    cv_v = cache_v[0, 0].rearrange("t h d -> t (h d)")
    nks_v = new_k_s[0, 0].rearrange("t h d -> t (h d)")
    nvs_v = new_v_s[0, 0].rearrange("t h d -> t (h d)")
    nkp_v = new_k_p[0, 0].rearrange("(t p) h d -> p t (h d)", p=P)
    nvp_v = new_v_p[0, 0].rearrange("(t p) h d -> p t (h d)", p=P)

    ctx = ExitStack()
    with ctx:
        WB = KC * D
        ZONE = 5 * WB
        SB = ctx.enter_context(nc.sbuf_tensor("SB", [P, ZONE + 12200], F32))
        PS = ctx.enter_context(nc.psum_tensor("PS", [P, 8, 512], F32))

        def view(off, *dims, rows=P):
            n = 1
            for d in dims:
                n *= d
            ap = SB[0:rows, off:off + n]
            if len(dims) == 2:
                ap = ap.rearrange("p (a b) -> p a b", a=dims[0])
            if len(dims) == 3:
                ap = ap.rearrange("p (a b c) -> p a b c", a=dims[0], b=dims[1])
            return ap

        def view16(off, dt, *dims, rows=P):
            n = 1
            for d in dims:
                n *= d
            ap = SB[0:rows, off:off + (n + 1) // 2].bitcast(dt)
            if len(dims) == 2:
                ap = ap.rearrange("p (a b) -> p a b", a=dims[0])
            if len(dims) == 3:
                ap = ap.rearrange("p (a b c) -> p a b c", a=dims[0], b=dims[1])
            return ap

        wbuf = [view(i * WB, KC, D) for i in range(5)]
        WG, WU, WD = (wbuf[0], wbuf[3]), (wbuf[1], wbuf[4]), wbuf[2]
        ring = [view(s * 4096, KC, 512) for s in range(2)]
        qpad = [view(WB + h * 2560, KC, T) for h in range(2)]
        kT = view(WB + 5120, KC, T)
        parT = view(WB + 7680, 80)
        dwT = view(WB + 7760, KC, KW)
        mean_w = view(WB + 8008, P)
        yc = view(2 * WB, KC, CONVN)
        sq = view(2 * WB, KC, T)
        rstd_c = view(2 * WB + 2800, T)
        relb = view(2 * WB, H, 2 * P)
        bv_bc = view(2 * WB + 4096, D)
        probs = [view(2 * WB + 4096 + i * 1152, 1152) for i in range(2)]
        ck_tok = view(2 * WB + 6400, D)
        ln1g_bc, ln1b_bc = view(2 * WB, D), view(2 * WB + D, D)
        xtok = view(3 * WB, 3, D)
        vtok = view(3 * WB + 3072, 3, D)
        cv_tok = view(3 * WB + 6144, D)
        ckT = view(3 * WB + 7168, KC, P)
        bdown_sb = view(3 * WB + 3072, D, rows=E)
        gT = view(3 * WB + 6144, T, rows=E)
        ua = view(4 * WB, KC, T)
        zc = ua
        ga = view(4 * WB + 2560, KC, T)
        gb = view(4 * WB + 5120, KC, T)
        braw = view(4 * WB + 2560, 2, D, rows=96)
        resid = view(4 * WB, 3, D)
        wr = view(4 * WB + 7680, KC, E)
        br_bc = view(4 * WB + 7936, E)
        xT = view(ZONE, KC, T)
        mixT = xT
        ub = view(ZONE + 2560, KC, T)
        oT = ub
        uext = view(ZONE + 5120, KC, UEXT)
        ktok = view(ZONE + 5120, 3, D)
        bout_bc = view(ZONE + 8192, D)
        convout = view(ZONE + 8192, 2, D, rows=HALO)
        pT = [view(ZONE + 8192 + i * 1024, 1024) for i in range(2)]
        xh = view16(ZONE, BF16, 3, 3, D)
        yacc = view(ZONE + 4608, KC, T)
        xg = view(ZONE + 7168, KC, SLOTS)
        gmin = view(ZONE + 7680, 512)
        hT = view(ZONE + 7680, 4, 2, SLOTS)
        hT_small = view(ZONE + 7680, 2, 4, SMALL)
        act_h = view(ZONE + 8192, 512)
        ysb = view(ZONE + 8704, 512)
        scat = [view(ZONE + 9216 + h * T, T) for h in range(2)]
        sgate = view(ZONE + 9856, 3, SLOTS)
        sel = view16(ZONE + 10048, BF16, 3, SLOTS)
        bsel = view16(ZONE + 10144, BF16, SLOTS, rows=96)
        K0 = ZONE + 10240
        bparts = view16(K0, BF16, 2, D, rows=96)
        ident = view(K0 + 1024, P)
        iota = view16(K0 + 1152, F16, T)
        onehot = view16(K0 + 1312, BF16, E, rows=96)
        eps_c = view(K0 + 1328, 1)
        tbl = view(K0 + 1330, 34, rows=1).bitcast(I32)
        gates = view(K0 + 1364, 3, E)
        rank = view(K0 + 1460, 3, E)
        sm = K0 + 1556
        stats = view(sm, 3, 12)
        mv = view(sm + 36, 3, 2)
        rstd = view(sm + 42, 3)
        nmax = view(sm + 48, 12)
        psumr = view(sm + 60, 12)
        rsum = view(sm + 72, 12)
        nblk = view(sm + 84, E, rows=1).bitcast(I32)
        dist = view(sm + 116, 3, SLOTS)
        tail = view(sm + 308, E, rows=1).bitcast(I32)
        order = view(sm + 340, E, rows=1).bitcast(I32)
        R0 = ZONE + 7680
        lg = view(R0, 3, E)
        top8 = view(R0 + 96, 3, 8)
        idx8 = view(R0 + 120, 3, 8).bitcast(U32)
        idxf = view(R0 + 144, 3, 8)
        e4 = view(R0 + 168, 3, 4)
        ssum = view(R0 + 180, 3)
        rs4 = view(R0 + 184, 3)
        ntop = view(R0 + 188, 3)
        term = view(R0 + 192, 3, TOPK, E)
        chosen = view16(R0 + 576, BF16, 3, E)
        tri = view16(R0 + 624, BF16, P)
        ones16 = view16(R0 + 688, BF16, P)
        cnt = view(R0 + 752, E, rows=1)
        nb = view(R0 + 784, E, rows=1)
        cum = view(R0 + 816, E, rows=1)
        one_r = view(R0 + 848, E, rows=1)
        small = view(R0 + 880, E, rows=1)
        R1 = ZONE + 9856
        key = view(R1, E, rows=E)
        diag = view(R1 + 32, 3, E, rows=E)
        cols = view(R1 + 128, 3, rows=E)
        place = view(R1 + 132, 1, rows=E)
        at_place = view(R1 + 136, E, rows=E)
        tie = view(R1 + 168, E, rows=E)
        par_rows = view(ZONE + 2560, P, rows=80)
        dw_rows = view(ZONE + 2560 + P, D, rows=KW)
        st_rows = view(ZONE + 2560 + P + D, D, rows=HALO)
        rb_sb = view(2 * WB, NREL, rows=H)
        rev_sb = view(2 * WB + NREL, REV, rows=H)

        def psv(bank, n, a=None):
            ap = PS[:, bank, 0:n]
            return ap

        sems = {}

        def sem(name):
            if name not in sems:
                sems[name] = ctx.enter_context(nc.semaphore(name))
            return sems[name]

        def apart(eng):
            eng.wait_ge(sem("tables_done"), 1)

        def load_by(eng, buf, src, name):
            for h in range(2):
                eng.dma_start(buf[:, 4 * h:4 * h + 4, :], src[:, 4 * h:4 * h + 4, :]).then_inc(sem(f"{name}_{h}"), 16)

        def weights(v, e):
            return v[bass.ds(e, 1)].rearrange("a p c n -> p (a c) n")

        block = ctx.enter_context(nc.Block())

        @block.sync
        def _(sp):
            sp.dma_start(xtok[:, 0:2, :], x_prompt[0].rearrange("(t p) n -> p t n", p=P)).then_inc(sem("x_in"), 16)
            sp.dma_start(xtok[0:NS_, 2, :], x_sample[0]).then_inc(sem("x_in"), 16)
            sp.dma_start(par_rows[0:56, :], b_in.rearrange("a (c p) -> (a c) p", p=P)).then_inc(sem("par_in"), 16)
            sp.dma_start(par_rows[56:64, :], b_dw.rearrange("a (c p) -> (a c) p", p=P)).then_inc(sem("par_in"), 16)
            sp.dma_start(par_rows[64:72, :], conv_ln_g.rearrange("a (c p) -> (a c) p", p=P)).then_inc(sem("par_in"), 16)
            sp.dma_start(par_rows[72:80, :], conv_ln_b.rearrange("a (c p) -> (a c) p", p=P)).then_inc(sem("par_in"), 16)
            sp.dma_start(dw_rows, w_dw[0]).then_inc(sem("par_in"), 16)
            sp.dma_start(st_rows, state_conv[0, 0]).then_inc(sem("par_in"), 16)
            for s in range(2):
                sp.dma_start(ring[s], w_in_v[:, :, 3, s, :]).then_inc(sem(f"ring{s}"), 16)
            sp.dma_start(ck_tok, ck_v).then_inc(sem("ck_in"), 16)
            sp.dma_start(cv_tok, cv_v).then_inc(sem("cv_in"), 16)
            sp.dma_start(bv_bc, b_in[:, 2 * D:3 * D].broadcast_to([P, D])).then_inc(sem("bv_in"), 16)
            sp.dma_start(bout_bc, b_out.broadcast_to([P, D])).then_inc(sem("bout_in"), 16)
            sp.dma_start(rb_sb, rel_bias[0]).then_inc(sem("rb_in"), 16)
            for g in range(3):
                sp.dma_start(braw[32 * g:32 * g + 32, 0, :], b_gate[0]).then_inc(sem("braw_in"), 16)
                sp.dma_start(braw[32 * g:32 * g + 32, 1, :], b_up[0]).then_inc(sem("braw_in"), 16)
            sp.dma_start(wr, rows(w_router)).then_inc(sem("wr_in"), 16)
            sp.dma_start(br_bc, b_router.broadcast_to([P, E])).then_inc(sem("wr_in"), 16)
            sp.wait_ge(sem("rev_done"), 1)
            sp.dma_start(bass.AP(tensor=rev_dram.tensor, offset=0, ap=[[REV, H], [BROW + 1, P], [1, REV]]),
                         rev_sb.rearrange("h (a n) -> h a n", a=1).broadcast_to([H, P, REV])).then_inc(sem("rev_out"), 16)

            def group(s, src, user, count):
                sp.wait_ge(sem(user), count)
                sp.dma_start(ring[s], src).then_inc(sem(f"ring{s}"), 16)

            with sp.Fori(1, 4) as i:
                for s in range(2):
                    group(s, w_in_v[:, :, bass.ds(i + 3, 1), s, :].rearrange("p c a n -> p c (a n)"), "proj_mm", i * 8 + (4 * s - 4))
            with sp.Fori(4, 6) as i:
                for s in range(2):
                    group(s, w_in_v[:, :, bass.ds(i - 4, 1), s, :].rearrange("p c a n -> p c (a n)"), "proj_mm", i * 8 + (4 * s - 4))
            for s in range(2):
                group(s, w_in_v[:, :, 2, s, :], "proj_mm", 44 + 4 * s)
            sp.wait_ge(sem("rev_out"), 16)
            sp.wait_ge(sem("z_ready"), KC)
            src = bass.AP(tensor=rev_dram.tensor, offset=P - 1, ap=[[BROW, P], [REV, H], [1, 2 * P]])
            sp.dma_start(relb, src).then_inc(sem("relb_in"), 16)
            for s in range(2):
                group(s, w_pw_v[:, :, s, :], "v_mm", 3 * (s + 1))
            for s in range(2):
                group(s, w_att_v[:, :, s, :], "pw_mm", 4 * (s + 1))
            sp.wait_ge(sem("probs_ready"), PAIRS)
            sp.dma_start(ln1g_bc, ln1_g.broadcast_to([P, D])).then_inc(sem("ln1_in"), 16)
            sp.dma_start(ln1b_bc, ln1_b.broadcast_to([P, D])).then_inc(sem("ln1_in"), 16)
            sp.wait_ge(sem("o_mm"), PAIRS)
            sp.wait_ge(sem("v_out"), 32)
            sp.dma_start(bdown_sb, b_down[0]).then_inc(sem("bdown_in"), 16)
            for s in range(2):
                group(s, w_out_v[:, :, s, :], "ao_mm", 4 * (s + 1))

            def load(buf, src, name):
                load_by(sp, buf, src, name)

            sp.wait_ge(sem("ktok_mm"), 6)
            load(WU[0], wu_v[0], "wu0")
            sp.wait_ge(sem("out_mm"), 6)
            load(WG[0], wg_v[0], "wg0")
            sp.wait_ge(sem("x1_ready"), 3)
            load(WD, wd_v[0], "wd")
            sp.wait_ge(sem("lo_ready"), 3)
            sp.wait_ge(sem("tables_done"), 1)
            load(WU[1], wu_v[1], "wu1")
            sp.wait_ge(sem("bias_mm"), KC)
            load(WG[1], wg_v[1], "wg1")

            def expert_at(place):
                return sp.value_load(order[0:1, bass.ds(place, 1)], min_val=0, max_val=E - 1)

            with sp.Fori(1, E // 2) as q:
                for par in range(2):
                    first = sp.value_load(tbl[0:1, bass.ds(q * 2 + (par - 1), 1)], min_val=1, max_val=200)
                    e = expert_at(q * 2 + par)
                    sp.wait_ge(sem("gate_done"), first)
                    load(WG[par], weights(wg_v, e), f"wg{par}")
                    sp.wait_ge(sem("up_done"), first + 1)
                    load(WU[par], weights(wu_v, e), f"wu{par}")
            last = sp.value_load(tbl[0:1, E - 1:E], min_val=1, max_val=200)
            sp.wait_ge(sem("up_done"), last + 1)
            sp.dma_start(WG[0][:, 0, :], ln2_g.broadcast_to([P, D])).then_inc(sem("ln2_in"), 16)
            sp.dma_start(WG[0][:, 1, :], ln2_b.broadcast_to([P, D])).then_inc(sem("ln2_in"), 16)
            for tt in range(2):
                sp.wait_ge(sem("y_ready"), tt + 1)
                sp.dma_start(y_prompt[0, P * tt:P * tt + P, :], WG[0][:, 2 + tt, :]).then_inc(sem("y_out"), 16)
            sp.wait_ge(sem("y_ready"), 3)
            sp.dma_start(y_sample[0], WG[0][0:NS_, 4, :]).then_inc(sem("y_out"), 16)
            sp.wait_ge(sem("y_out"), 48)

        @block.gpsimd
        def _(pool):
            n = [0]

            def link(ins):
                n[0] += 1
                ins.then_inc(sem("pool_chain"), 1)
                pool.wait_ge(sem("pool_chain"), n[0])

            pool.sem_inc(sem("proj_evac"), 4)
            for name in ("sel_ready", "sgate_ready", "gather_done", "scat_mm", "up_done", "hT_ready"):
                pool.sem_inc(sem(name), 1)
            link(pool.memset(ident, 0.0))
            pool.affine_select(ident, ident, pattern=[[-1, P]], compare_op=ALU.not_equal, fill=1.0,
                               base=0, channel_multiplier=1).then_inc(sem("ident_ready"), 1)
            pool.memset(mean_w, 1.0 / D).then_inc(sem("consts"), 1)
            pool.memset(eps_c, EPS).then_inc(sem("consts"), 1)
            pool.memset(uext[:, :, 0:HALO], 0.0).then_inc(sem("uext_zero"), 1)
            pool.wait_ge(sem("uext_zero"), 1)
            pool.memset(qpad[0][64:128], 0.0).then_inc(sem("qpad_zero"), 1)
            pool.wait_ge(sem("qpad_zero"), 1)
            pool.memset(qpad[1][0:64], 0.0).then_inc(sem("qpad_zero"), 1)
            pool.wait_ge(sem("qpad_zero"), 2)
            pool.iota(iota, [[1, T]], base=0, channel_multiplier=0,
                      allow_small_or_imprecise_dtypes=True).then_inc(sem("iota_ready"), 1)
            pool.wait_ge(sem("ident_ready"), 1)
            pool.wait_ge(sem("iota_ready"), 1)
            for g in range(3):
                s = slice(32 * g, 32 * g + 32)
                pool.tensor_copy(onehot[s, :], ident[s, s]).then_inc(sem("onehot_ready"), 1)
                pool.wait_ge(sem("onehot_ready"), g + 1)
            pool.wait_ge(sem("xT_mm"), KC)
            pool.wait_ge(sem("bout_in"), 16)
            for tt, (_, r) in enumerate(TT):
                link(pool.tensor_scalar(xtok[0:r, tt, :], xtok[0:r, tt, :], ALPHA, None, ALU.mult))
                pool.tensor_tensor(xtok[0:r, tt, :], xtok[0:r, tt, :], bout_bc[0:r], ALU.add).then_inc(sem("xr_ready"), 1)
                pool.wait_ge(sem("xr_ready"), tt + 1)
            pool.wait_ge(sem("braw_in"), 96)
            link(pool.tensor_copy(bparts, braw))
            link(pool.tensor_tensor(braw, braw, bparts, ALU.subtract))
            pool.tensor_copy(bparts[32:64], braw[32:64]).then_inc(sem("bparts_ready"), 1)
            pool.wait_ge(sem("bparts_ready"), 1)
            link(pool.tensor_copy(bparts[64:96], braw[64:96]))
            link(pool.tensor_tensor(braw[64:96], braw[64:96], bparts[64:96], ALU.subtract))
            pool.tensor_copy(bparts[64:96], braw[64:96]).then_inc(sem("bparts_ready"), 1)
            pool.dma_start(nks_v[0:PAST - NS_], ck_v[NS_:PAST]).then_inc(sem("kv_out"), 16)
            pool.dma_start(nvs_v[0:PAST - NS_], cv_v[NS_:PAST]).then_inc(sem("kv_out"), 16)
            pool.wait_ge(sem("convout_ready"), 4)
            pool.dma_start(new_conv_p[0, 0], convout[:, 0, :]).then_inc(sem("conv_out"), 16)
            pool.dma_start(new_conv_s[0, 0], convout[:, 1, :]).then_inc(sem("conv_out"), 16)
            pool.wait_ge(sem("v_ready"), 6)
            pool.dma_start(nvp_v, vtok[:, 0:2, :]).then_inc(sem("v_out"), 16)
            pool.dma_start(nvs_v[PAST - NS_:PAST], vtok[0:NS_, 2, :]).then_inc(sem("v_out"), 16)
            pool.wait_ge(sem("ktok_ready"), 6)
            pool.dma_start(nkp_v, ktok[:, 0:2, :]).then_inc(sem("k_out"), 16)
            pool.dma_start(nks_v[PAST - NS_:PAST], ktok[0:NS_, 2, :]).then_inc(sem("k_out"), 16)
            pool.wait_ge(sem("k_out"), 32)
            link(pool.memset(tri, 1.0))
            pool.affine_select(tri, tri, pattern=[[1, P]], compare_op=ALU.is_ge, fill=0.0,
                               base=0, channel_multiplier=-1).then_inc(sem("tri_ready"), 1)
            pool.memset(ones16, 1.0).then_inc(sem("tri_ready"), 1)
            pool.wait_ge(sem("tri_ready"), 2)
            pool.wait_ge(sem("x1_ready"), 3)
            for part in range(3):
                pool.memset(xh[64:128, part, 2, :], 0.0).then_inc(sem("xh_zero"), 1)
                pool.wait_ge(sem("xh_zero"), part + 1)
            pool.memset(scat[0], 0.0).then_inc(sem("scat_ready"), 1)
            pool.memset(scat[1], 0.0).then_inc(sem("scat_ready"), 1)
            pool.memset(ysb, 0.0).then_inc(sem("y_sb"), 1)
            pool.wait_ge(sem("y_sb"), 1)

            pool.wait_ge(sem("tables_done"), 1)
            pool.wait_ge(sem("onehot_ready"), 3)

            with pool.Fori(0, E) as k:
                first = pool.value_load(tbl[0:1, bass.ds(k, 1)], min_val=0, max_val=200)
                blocks = pool.value_load(nblk[0:1, bass.ds(k, 1)], min_val=1, max_val=T // SLOTS)
                e = pool.value_load(order[0:1, bass.ds(k, 1)], min_val=0, max_val=E - 1)
                apart(pool)
                pool.wait_ge(sem("up_done"), first + 1)
                pool.wait_ge(sem("sgate_ready"), first + 1)
                pool.tensor_copy(bsel, onehot[:, bass.ds(e, 1)].broadcast_to([96, SLOTS])).then_inc(sem("bsel_ready"), 1)
                with pool.Fori(0, blocks) as b:
                    i = first + b
                    apart(pool)
                    pool.wait_ge(sem("bsel_ready"), k + 1)
                    pool.wait_ge(sem("sel_ready"), i + 1)
                    pool.tensor_tensor(dist, iota[:, bass.ds(b * SLOTS, SLOTS)].rearrange("p (a s) -> p a s", a=1).broadcast_to([P, 3, SLOTS]),
                                       rank[:, :, bass.ds(e, 1)].broadcast_to([P, 3, SLOTS]),
                                       ALU.subtract).then_inc(sem("dist_ready"), 1)
                    apart(pool)
                    pool.wait_ge(sem("dist_ready"), i + 1)
                    pool.wait_ge(sem("gather_done"), i + 1)
                    pool.tensor_scalar(sel, dist, 0.0, None, ALU.is_equal).then_inc(sem("sel_ready"), 1)
                    pool.wait_ge(sem("scat_mm"), i + 1)
                    pool.wait_ge(sem("sel_ready"), i + 2)
                    pool.tensor_tensor(sgate, sel, gates[:, :, bass.ds(e, 1)].broadcast_to([P, 3, SLOTS]),
                                       ALU.mult).then_inc(sem("sgate_ready"), 1)
            total = pool.value_load(tbl[0:1, E:E + 1], min_val=1, max_val=200)
            pool.wait_ge(sem("gather_done"), total + 1)
            pool.tensor_tensor(sel, sel, sel, ALU.subtract).then_inc(sem("sel_ready"), 1)
            pool.wait_ge(sem("kv_out"), 32)
            pool.wait_ge(sem("conv_out"), 32)
            pool.wait_ge(sem("v_out"), 32)

        @block.scalar
        def _(act):
            act.wait_ge(sem("par_ready"), 1)
            def tile(i, s, t, dst, func, col):
                act.wait_ge(sem("proj_mm"), i * 8 + (s * 4 + t + 1))
                c = s * 4 + t
                act.activation(dst[:, bass.ds(c, 1), :].rearrange("p a n -> p (a n)"), PS[:, t, 0:T], func,
                               bias=parT[:, bass.ds(col + c, 1)]).then_inc(sem("proj_evac"), 1)

            for i, (dst, func, col) in enumerate([(ua, ACT.Identity, 24), (ub, ACT.Sigmoid, 32),
                                                  (ga, ACT.Sigmoid, 40), (gb, ACT.Sigmoid, 48)]):
                if i == 2:
                    act.wait_ge(sem("bparts_ready"), 2)
                with act.Fori(0, 2) as s:
                    for t in range(4):
                        tile(i, s, t, dst, func, col)
            for b in range(4):
                act.wait_ge(sem("convout_mm"), b + 1)
                if b == 0:
                    act.wait_ge(sem("xr_ready"), 3)
                act.copy(convout[:, b // 2, (b % 2) * 512:(b % 2) * 512 + 512],
                         PS[0:HALO, 4 + b, 0:512]).then_inc(sem("convout_ready"), 1)
            act.wait_ge(sem("qpad_zero"), 2)
            with act.Fori(0, 2) as s:
                for t in range(4):
                    act.wait_ge(sem("proj_mm"), s * 4 + (32 + t + 1))
                    for h in range(2):
                        r = slice(64 * h, 64 * h + 64)
                        ins = act.activation(qpad[h][r, bass.ds(s * 4 + t, 1), :].rearrange("p a n -> p (a n)"), PS[r, t, 0:T],
                                             ACT.Identity, bias=parT[r, bass.ds(s * 4 + t, 1)])
                    ins.then_inc(sem("proj_evac"), 1)
            with act.Fori(0, 2) as s:
                for t in range(4):
                    tile(5, s, t, kT, ACT.Identity, 8)
            act.wait_ge(sem("zc_centred"), 2)
            act.activation(sq, zc, ACT.Square).then_inc(sem("sq_ready"), 1)
            act.wait_ge(sem("var_mm"), 1)
            act.wait_ge(sem("consts"), 2)
            act.activation(rstd_c, PS[:, 5, 0:T], ACT.Sqrt, bias=eps_c).then_inc(sem("std_c"), 1)
            act.wait_ge(sem("z_norm"), 1)
            for c in range(KC):
                act.activation(zc[:, c, :], zc[:, c, :], ACT.Silu, bias=parT[:, 72 + c:73 + c],
                               scale=parT[:, 64 + c:65 + c]).then_inc(sem("z_ready"), 1)

            def exps(j):
                pr = probs[j % 2]
                act.wait_ge(sem("scores_ready"), j + 1)
                k = 6 * (j % 2)
                for a, (o, w, r) in enumerate([(0, 256, 128), (256, 256, 128), (512, 128, 128), (640, 128, 128),
                                               (768, 192, 64), (960, 192, 64)]):
                    ins = act.activation(pr[0:r, o:o + w], pr[0:r, o:o + w], ACT.Exp, bias=nmax[0:r, k + a:k + a + 1],
                                         accum_out=psumr[0:r, k + a:k + a + 1])
                ins.then_inc(sem("exp_done"), 1)

            def evac_p(j):
                pt = pT[j % 2]
                act.wait_ge(sem("p_mm"), j + 1)
                if j == 0:
                    act.wait_ge(sem("conv_out"), 32)
                act.copy(pt[:, 0:512], PS[:, 3, :])
                act.copy(pt[:, 512:896], PS[:, 4, 0:384])
                act.copy(pt[0:64, 896:1024], PS[0:64, 4, 384:512]).then_inc(sem("pT_ready"), 1)

            def evac_o(j):
                act.wait_ge(sem("o_mm"), j + 1)
                act.copy(oT[:, j, :], PS[:, 5, 0:T]).then_inc(sem("o_ready"), 1)

            for j in range(PAIRS):
                exps(j)
                if j >= 1:
                    evac_o(j - 1)
                evac_p(j)
            evac_o(PAIRS - 1)
            for b in range(6):
                tt, half = b // 2, b % 2
                r = TT[tt][1]
                act.wait_ge(sem("ktok_mm"), b + 1)
                act.copy(ktok[0:r, tt, half * 512:half * 512 + 512], PS[0:r, 4 + b % 4, :]).then_inc(sem("ktok_ready"), 1)
            act.wait_ge(sem("var1"), 1)
            act.activation(rstd, mv[:, :, 1], ACT.Sqrt, bias=eps_c).then_inc(sem("std1"), 1)
            for tt, (_, r) in enumerate(TT):
                act.wait_ge(sem("x1_ready"), tt + 1)
                if tt == 0:
                    act.wait_ge(sem("k_out"), 32)
                act.copy(xh[0:r, 0, tt, :], xtok[0:r, tt, :]).then_inc(sem("hi_ready"), 1)
            for tt, (_, r) in enumerate(TT):
                act.wait_ge(sem("resid1"), tt + 1)
                act.copy(xh[0:r, 1, tt, :], resid[0:r, tt, :]).then_inc(sem("mid_ready"), 1)
            for c in range(1, KC, 2):
                act.wait_ge(sem("x1T_mm"), c + 1)
                act.copy(yacc[:, c, :], PS[:, c, 0:T]).then_inc(sem("x1T_a"), 1)
            for tt, (_, r) in enumerate(TT):
                act.wait_ge(sem("top_ready"), tt + 1)
                act.activation(e4[0:r, tt, :], top8[0:r, tt, 0:4], ACT.Exp, bias=ntop[0:r, tt:tt + 1],
                               accum_out=ssum[0:r, tt:tt + 1]).then_inc(sem("e4_ready"), 1)

            act.wait_ge(sem("tables_done"), 1)
            act.wait_ge(sem("gather_done"), 2)
            act.copy(xg, PS[:, 2, :].rearrange("p (c s) -> p c s", c=KC)).then_inc(sem("xg_ready"), 1)

            def expert_block(i, n):
                act.wait_ge(sem("gmin_ready"), i + 1)
                act.activation(act_h[:, 0:n], gmin[:, 0:n], ACT.Sigmoid, scale=SW_ALPHA).then_inc(sem("sig_ready"), 1)
                act.wait_ge(sem("gather_done"), i + 3)
                act.copy(xg, PS[:, 2, :].rearrange("p (c s) -> p c s", c=KC)).then_inc(sem("xg_ready"), 1)
                act.wait_ge(sem("down_done"), i + 1)
                act.copy(ysb, PS[:, 5, :]).then_inc(sem("y_sb"), 1)

            def expert(k, e_next):
                first = act.value_load(tbl[0:1, bass.ds(k, 1)], min_val=0, max_val=200)
                full = act.value_load(tail[0:1, bass.ds(k, 1)], min_val=0, max_val=200)
                end = act.value_load(tbl[0:1, bass.ds(k + 1, 1)], min_val=1, max_val=200)
                with act.If(first < full):
                    with act.Fori(first, full) as i:
                        expert_block(i, 512)
                with act.If(full < end):
                    with act.Fori(full, end) as i:
                        expert_block(i, 256)
                if e_next is not None:
                    load_by(act, WD, weights(wd_v, e_next), "wd")

            with act.Fori(0, E - 1) as k:
                expert(k, act.value_load(order[0:1, bass.ds(k + 1, 1)], min_val=0, max_val=E - 1))
            expert(E - 1, None)
            act.wait_ge(sem("var2"), 1)
            act.activation(rstd, mv[:, :, 1], ACT.Sqrt, bias=eps_c).then_inc(sem("std2"), 1)

        @block.vector
        def _(dve):
            n = [0]

            def link(ins):
                n[0] += 1
                ins.then_inc(sem("dve_chain"), 1)
                dve.wait_ge(sem("dve_chain"), n[0])

            dve.wait_ge(sem("par_mm"), 1)
            dve.tensor_copy(parT, PS[:, 4, 0:80]).then_inc(sem("par_ready"), 1)
            for c in range(KC):
                dve.wait_ge(sem("xT_mm"), c + 1)
                dve.tensor_copy(xT[:, c, :], PS[:, c % 4, 0:T]).then_inc(sem("xT_ready"), 1)
            dve.wait_ge(sem("dw_mm"), 1)
            link(dve.tensor_copy(dwT, PS[:, 5, 0:KC * KW].rearrange("p (c k) -> p c k", c=KC)))
            dve.wait_ge(sem("state_mm"), 1)
            dve.tensor_copy(uext[:, :, HALO + NP_:US], PS[:, 6, 0:KC * HALO].rearrange("p (c k) -> p c k", c=KC))\
               .then_inc(sem("state_ready"), 1)
            dve.wait_ge(sem("rb_in"), 16)
            dve.tensor_copy(rev_sb[:, 0:MAXREL - 1], rb_sb[:, NREL - 1:NREL].broadcast_to([H, MAXREL - 1]))
            dve.memset(rev_sb[:, REV - 1:REV], 0.0)
            dve.tensor_copy(rev_sb[:, MAXREL - 1:REV - 1], rb_sb[:, NREL - 1:0:-1]).then_inc(sem("rev_done"), 1)
            for h in range(2):
                dve.wait_ge(sem("ck_mm"), h + 1)
                dve.tensor_copy(ckT[:, 4 * h:4 * h + 4, :], PS[:, 7 - 3 * h, :].rearrange("p (c k) -> p c k", c=4))\
                   .then_inc(sem("ckT_ready"), 1)
            link(dve.memset(mv[:, :, :], 1.0))
            link(dve.memset(psumr[:, :], 1.0))
            dve.wait_ge(sem("uext_zero"), 1)
            for c in range(KC):
                dve.wait_ge(sem("proj_evac"), 4 + 8 + c + 1)
                dve.tensor_tensor(uext[:, c, HALO:HALO + NP_], ua[:, c, 0:NP_], ub[:, c, 0:NP_], ALU.mult).then_inc(sem("u_ready"), 1)
                dve.tensor_tensor(uext[:, c, US:US + NS_], ua[:, c, NP_:T], ub[:, c, NP_:T], ALU.mult).then_inc(sem("u_ready"), 1)
            dve.wait_ge(sem("u_ready"), 2 * KC)
            dve.wait_ge(sem("rev_out"), 16)
            for c in range(KC):
                dve.tensor_scalar(yc[:, c, :], uext[:, c, 0:CONVN], dwT[:, c, 0:1], parT[:, 56 + c:57 + c],
                                  ALU.mult, ALU.add).then_inc(sem("conv"), 1)
            with dve.Fori(1, KW) as k:
                for c in range(KC):
                    dve.wait_ge(sem("conv"), k * KC + (c + 1 - KC))
                    dve.scalar_tensor_tensor(
                        yc[:, c, :], uext[:, c, bass.ds(k, CONVN)],
                        dwT[:, c, bass.ds(k, 1)], yc[:, c, :], ALU.mult, ALU.add).then_inc(sem("conv"), 1)
            dve.wait_ge(sem("mean_mm"), 1)

            def over_chunks(ap, n):
                return ap.rearrange("p (a n) -> p a n", a=1).broadcast_to([P, KC, n])

            dve.tensor_tensor(zc[:, :, 0:NP_], yc[:, :, 0:NP_], over_chunks(PS[:, 4, 0:NP_], NP_),
                              ALU.subtract).then_inc(sem("zc_centred"), 1)
            dve.tensor_tensor(zc[:, :, NP_:T], yc[:, :, NP_ + HALO:CONVN], over_chunks(PS[:, 4, NP_ + HALO:CONVN], NS_),
                              ALU.subtract).then_inc(sem("zc_centred"), 1)
            dve.wait_ge(sem("bv_in"), 16)

            def values(s):
                for tt, (_, r) in enumerate(TT):
                    dve.wait_ge(sem("v_mm"), 3 * s + tt + 1)
                    dve.tensor_tensor(vtok[0:r, tt, 512 * s:512 * s + 512], PS[0:r, [0, 1, 2, 3, 6, 7][3 * s + tt], :],
                                      bv_bc[0:r, 512 * s:512 * s + 512], ALU.add).then_inc(sem("v_ready"), 1)

            values(0)
            dve.wait_ge(sem("std_c"), 1)
            link(dve.reciprocal(rstd_c, rstd_c))
            dve.tensor_tensor(zc, zc, over_chunks(rstd_c, T), ALU.mult).then_inc(sem("z_norm"), 1)
            values(1)

            def score(j):
                pr = probs[j % 2]
                k = 6 * (j % 2)
                dve.wait_ge(sem("score_mm"), j + 1)
                if j == 0:
                    dve.wait_ge(sem("relb_in"), 16)
                    link(dve.memset(relb[0:64, :, 192:256], NEG))
                for o, w, r, bank, b0 in [(0, 256, 128, 0, 0), (512, 128, 128, 1, 128), (768, 192, 64, 2, 0)]:
                    ins = dve.scalar_tensor_tensor(
                        pr[0:r, o:o + 2 * w].rearrange("p (h k) -> p h k", h=2),
                        PS[0:r, bank, 0:2 * w].rearrange("p (h k) -> p h k", h=2), SCALE,
                        relb[0:r, 2 * j:2 * j + 2, b0:b0 + w], ALU.mult, ALU.add)
                link(ins)
                for a, (o, w, r) in enumerate([(0, 256, 128), (512, 128, 128), (768, 192, 64)]):
                    ins = dve.tensor_reduce(nmax[0:r, k + 2 * a:k + 2 * a + 2],
                                            pr[0:r, o:o + 2 * w].rearrange("p (h k) -> p h k", h=2),
                                            AXX, ALU.max, negate=True)
                ins.then_inc(sem("scores_ready"), 1)

            def normalise(j):
                pr = probs[j % 2]
                k = 6 * (j % 2)
                dve.wait_ge(sem("exp_done"), j + 1)
                link(dve.reciprocal(rsum[:, k:k + 6], psumr[:, k:k + 6]))
                for a, (o, w, r) in enumerate([(0, 256, 128), (512, 128, 128), (768, 192, 64)]):
                    v = pr[0:r, o:o + 2 * w].rearrange("p (h k) -> p h k", h=2)
                    ins = dve.tensor_tensor(v, v, rsum[0:r, k + 2 * a:k + 2 * a + 2].rearrange("p (h a) -> p h a", a=1)
                                            .broadcast_to([r, 2, w]), ALU.mult)
                ins.then_inc(sem("probs_ready"), 1)

            score(0)
            for j in range(PAIRS):
                if j + 1 < PAIRS:
                    if j >= 1:
                        dve.wait_ge(sem("p_mm"), j)
                    score(j + 1)
                normalise(j)
                dve.wait_ge(sem("pw_mm"), j + 1)
                dve.tensor_tensor(mixT[:, j, :], PS[:, 6 + j % 2, 0:T], gb[:, j, :], ALU.mult).then_inc(sem("pw_evac"), 1)
            for t in range(KC):
                dve.wait_ge(sem("ao_mm"), t + 1)
                ins = dve.tensor_tensor(ga[:, t, :], PS[:, t % 4, 0:T], ga[:, t, :], ALU.mult)
                link(ins)
                dve.tensor_tensor(mixT[:, t, :], mixT[:, t, :], ga[:, t, :], ALU.add).then_inc(sem("mix_ready"), 1)
            dve.wait_ge(sem("xr_ready"), 3)
            for s in range(2):
                for tt, (_, r) in enumerate(TT):
                    dve.wait_ge(sem("out_mm"), 3 * s + tt + 1)
                    c = slice(512 * s, 512 * s + 512)
                    dve.tensor_tensor(xtok[0:r, tt, c], xtok[0:r, tt, c], PS[0:r, 3 * s + tt, :], ALU.add)\
                       .then_inc(sem("x1_pre"), 1)
                    dve.wait_ge(sem("x1_pre"), 3 * s + tt + 1)
                    ins = dve.bn_stats(stats[0:r, tt, 6 * s:6 * s + 6], xtok[0:r, tt, c])
            link(ins)
            for tt, (_, r) in enumerate(TT):
                ins = dve.bn_aggr(mv[0:r, tt, :], stats[0:r, tt, :])
            ins.then_inc(sem("var1"), 1)
            dve.wait_ge(sem("std1"), 1)
            link(dve.reciprocal(rstd, rstd))
            dve.wait_ge(sem("ln1_in"), 32)
            for tt, (_, r) in enumerate(TT):
                v = xtok[0:r, tt, :]
                link(dve.tensor_scalar(v, v, mv[0:r, tt, 0:1], rstd[0:r, tt:tt + 1], ALU.subtract, ALU.mult))
                link(dve.tensor_tensor(v, v, ln1g_bc[0:r], ALU.mult))
                dve.tensor_tensor(v, v, ln1b_bc[0:r], ALU.add).then_inc(sem("x1_ready"), 1)
            dve.wait_ge(sem("k_out"), 32)
            for c in range(0, KC, 2):
                dve.wait_ge(sem("x1T_mm"), c + 1)
                dve.tensor_copy(yacc[:, c, :], PS[:, c, 0:T]).then_inc(sem("x1T_d"), 1)
            for tt, (_, r) in enumerate(TT):
                dve.wait_ge(sem("hi_ready"), tt + 1)
                dve.tensor_tensor(resid[0:r, tt, :], xtok[0:r, tt, :], xh[0:r, 0, tt, :], ALU.subtract).then_inc(sem("resid1"), 1)
            for tt, (_, r) in enumerate(TT):
                dve.wait_ge(sem("mid_ready"), tt + 1)
                dve.tensor_tensor(xh[0:r, 2, tt, :], resid[0:r, tt, :], xh[0:r, 1, tt, :], ALU.subtract).then_inc(sem("lo_ready"), 1)

            link(dve.memset(gates, 0.0))
            link(dve.tensor_copy(tie, iota[0:E, 0:E]))
            link(dve.memset(tie[:, 0:1], -1e6))
            link(dve.memset(tie[:, 1:2], 1e6))
            dve.wait_ge(sem("logit_mm"), 1)
            dve.wait_ge(sem("wr_in"), 32)
            for tt, (_, r) in enumerate(TT):
                link(dve.tensor_tensor(lg[0:r, tt, :], PS[0:r, 0, E * tt:E * tt + E], br_bc[0:r], ALU.add))
                link(dve.max(top8[0:r, tt, :], lg[0:r, tt, :]))
                dve.tensor_scalar(ntop[0:r, tt:tt + 1], top8[0:r, tt, 0:1], -1.0, None, ALU.mult).then_inc(sem("top_ready"), 1)
                link(dve.max_index(idx8[0:r, tt, :], top8[0:r, tt, :], lg[0:r, tt, :]))
                link(dve.tensor_copy(idxf[0:r, tt, :], idx8[0:r, tt, :]))
            for tt, (_, r) in enumerate(TT):
                dve.wait_ge(sem("e4_ready"), tt + 1)
                link(dve.reciprocal(rs4[0:r, tt:tt + 1], ssum[0:r, tt:tt + 1]))
                link(dve.tensor_scalar(e4[0:r, tt, :], e4[0:r, tt, :], rs4[0:r, tt:tt + 1], None, ALU.mult))
                for k in range(TOPK):
                    ins = dve.tensor_scalar(term[0:r, tt, k, :], iota[0:r, 0:E], idxf[0:r, tt, k:k + 1],
                                            e4[0:r, tt, k:k + 1], ALU.is_equal, ALU.mult)
                link(ins)
                link(dve.tensor_tensor(term[0:r, tt, 0:2, :], term[0:r, tt, 0:2, :], term[0:r, tt, 2:4, :], ALU.add))
                link(dve.tensor_tensor(gates[0:r, tt, :], term[0:r, tt, 0, :], term[0:r, tt, 1, :], ALU.add))
            dve.tensor_scalar(chosen, gates, 0.0, None, ALU.is_gt).then_inc(sem("chosen_ready"), 1)
            dve.wait_ge(sem("rank_mm"), 1)
            dve.wait_ge(sem("chosen_ready"), 1)
            link(dve.tensor_tensor(rank, PS[:, 1, 0:3 * E].rearrange("p (t e) -> p t e", t=3), chosen, ALU.mult))
            link(dve.tensor_scalar(rank, rank, -1.0, None, ALU.add))
            total_row = PS[0:E, 1, 3 * E:4 * E]
            dve.scalar_tensor_tensor(key, total_row, 64.0, tie, ALU.mult, ALU.subtract)
            link(dve.tensor_tensor(diag[:, 1, :], total_row, ident[0:E, 0:E], ALU.mult))
            dve.tensor_tensor(diag[:, 2, :], iota[0:E, 0:E], ident[0:E, 0:E], ALU.mult)
            link(dve.tensor_tensor(diag[:, 0, :], key, ident[0:E, 0:E], ALU.mult))
            link(dve.tensor_reduce(cols, diag, AXX, ALU.add))
            link(dve.tensor_scalar(key, key, cols[:, 0:1], None, ALU.is_gt))
            link(dve.tensor_reduce(place, key, AXX, ALU.add))
            link(dve.tensor_scalar(key[:, 0:1], place, 2.0, None, ALU.mult))
            link(dve.tensor_scalar(place, place, -2.0, float(2 * E - 1), ALU.mult, ALU.add))
            link(dve.tensor_tensor(place, place, key[:, 0:1], ALU.min))
            dve.tensor_scalar(at_place, iota[0:E, 0:E], place, None, ALU.is_equal).then_inc(sem("at_place_ready"), 1)
            dve.wait_ge(sem("order_mm"), 1)
            link(dve.tensor_copy(order, PS[0:1, 2, E:2 * E]))
            link(dve.tensor_copy(cnt, PS[0:1, 2, 0:E]))
            link(dve.tensor_scalar(nb, cnt, float(SLOTS), 1.0, ALU.is_gt, ALU.add))
            for b in range(2, T // SLOTS):
                link(dve.scalar_tensor_tensor(nb, cnt, float(SLOTS * b), nb, ALU.is_gt, ALU.add))
            link(dve.memset(one_r, 1.0))
            link(dve.tensor_tensor_scan(cum, one_r, nb, 0.0, ALU.mult, ALU.add))
            link(dve.memset(tbl[:, 0:1], 0))
            link(dve.tensor_copy(nblk, nb))
            link(dve.scalar_tensor_tensor(small, nb, -float(SLOTS), cnt, ALU.mult, ALU.add))
            link(dve.tensor_scalar(small, small, float(SMALL - SLOTS), None, ALU.is_le))
            link(dve.tensor_tensor(small, cum, small, ALU.subtract))
            link(dve.tensor_copy(tail, small))
            dve.tensor_copy(tbl[:, 1:E + 1], cum).then_inc(sem("tables_done"), 1)
            dve.wait_ge(sem("gT_mm"), 1)
            dve.tensor_copy(gT, PS[0:E, 3, 0:T]).then_inc(sem("gT_ready"), 1)
            for c in range(KC):
                dve.wait_ge(sem("bias_mm"), c + 1)
                dve.scalar_tensor_tensor(yacc[:, c, :], yacc[:, c, :], ALPHA, PS[:, 4 + c % 4, 0:T], ALU.mult, ALU.add)\
                   .then_inc(sem("yacc"), 1)

            with dve.Fori(0, E) as e:
                first = dve.value_load(tbl[0:1, bass.ds(e, 1)], min_val=0, max_val=200)
                full = dve.value_load(tail[0:1, bass.ds(e, 1)], min_val=0, max_val=200)
                end = dve.value_load(tbl[0:1, bass.ds(e + 1, 1)], min_val=1, max_val=200)

                def expert_block(i, n):
                    dve.wait_ge(sem("gate_done"), i + 1)
                    dve.wait_ge(sem("hT_ready"), i + 1)
                    dve.tensor_scalar(gmin[:, 0:n], PS[:, 0, 0:n], LIMIT, None, ALU.min).then_inc(sem("gmin_ready"), 1)
                    dve.wait_ge(sem("sig_ready"), i + 1)
                    dve.tensor_tensor(act_h[:, 0:n], act_h[:, 0:n], gmin[:, 0:n], ALU.mult).then_inc(sem("gsig"), 1)
                    dve.wait_ge(sem("up_done"), i + 2)
                    dve.tensor_scalar(PS[:, 1, 0:n], PS[:, 1, 0:n], LIMIT, -LIMIT, ALU.min, ALU.max).then_inc(sem("upc"), 1)
                    dve.wait_ge(sem("gsig"), i + 1)
                    dve.wait_ge(sem("upc"), i + 1)
                    dve.scalar_tensor_tensor(act_h[:, 0:n], PS[:, 1, 0:n], 1.0, act_h[:, 0:n], ALU.add, ALU.mult).then_inc(sem("h_ready"), 1)
                    dve.wait_ge(sem("hT_mm"), i + 1)
                    if n == 512:
                        dve.tensor_copy(hT, PS[:, 3, :].rearrange("p (c h s) -> p c h s", c=4, h=2)).then_inc(sem("hT_ready"), 1)
                    else:
                        dve.tensor_copy(hT_small, PS[:, 3, 0:256].rearrange("p (c h s) -> p c h s", c=2, h=4)).then_inc(sem("hT_ready"), 1)
                    for c in range(KC):
                        dve.wait_ge(sem("comb_mm"), i * KC + (c + 1))
                        dve.tensor_tensor(yacc[:, c, :], yacc[:, c, :], PS[:, 6 + c % 2, 0:T], ALU.add).then_inc(sem("yacc"), 1)
                    dve.wait_ge(sem("scat_mm"), i + 2)
                    w = 64 * n // 512
                    for r in range(0, P, w):
                        ins = dve.tensor_copy(scat[r // 64][r:r + w], PS[0:w, 4, 0:T])
                    ins.then_inc(sem("scat_ready"), 1)

                with dve.If(first < full):
                    with dve.Fori(first, full) as i:
                        expert_block(i, 512)
                with dve.If(full < end):
                    with dve.Fori(full, end) as i:
                        expert_block(i, 256)
            total = dve.value_load(tbl[0:1, E:E + 1], min_val=1, max_val=200)
            for c in range(KC):
                dve.wait_ge(sem("comb_mm"), total * KC + (c + 1))
                dve.tensor_tensor(yacc[:, c, :], yacc[:, c, :], PS[:, 6 + c % 2, 0:T], ALU.add).then_inc(sem("yacc"), 1)
            for tt, (_, r) in enumerate(TT):
                for s in range(2):
                    dve.wait_ge(sem("y_mm"), 2 * tt + s + 1)
                    ins = dve.bn_stats(stats[0:r, tt, 6 * s:6 * s + 6], PS[0:r, 2 * tt + s, :])
            link(ins)
            for tt, (_, r) in enumerate(TT):
                ins = dve.bn_aggr(mv[0:r, tt, :], stats[0:r, tt, :])
            ins.then_inc(sem("var2"), 1)
            dve.wait_ge(sem("std2"), 1)
            link(dve.reciprocal(rstd, rstd))
            dve.wait_ge(sem("ln2_in"), 32)
            for tt, (_, r) in enumerate(TT):
                v = WG[0][0:r, 2 + tt, :]
                link(dve.tensor_scalar(v.rearrange("p (s n) -> p s n", s=2), PS[0:r, 2 * tt:2 * tt + 2, :], mv[0:r, tt, 0:1],
                                       rstd[0:r, tt:tt + 1], ALU.subtract, ALU.mult))
                link(dve.tensor_tensor(v, v, WG[0][0:r, 0, :], ALU.mult))
                dve.tensor_tensor(v, v, WG[0][0:r, 1, :], ALU.add).then_inc(sem("y_ready"), 1)

        @block.tensor
        def _(pe):
            def tr(out, in_):
                k = in_.shape[0]
                return pe.transpose(out, in_, ident[0:k, 0:k])

            pe.wait_ge(sem("ident_ready"), 1)
            pe.wait_ge(sem("par_in"), 96)
            tr(PS[:, 4, 0:80], par_rows).then_inc(sem("par_mm"), 1)
            pe.wait_ge(sem("x_in"), 32)
            for c in range(KC):
                if c >= 4:
                    pe.wait_ge(sem("xT_ready"), c - 3)
                for t0, r in TT:
                    ins = tr(PS[:, c % 4, t0:t0 + r], xtok[0:r, t0 // P, P * c:P * c + P])
                ins.then_inc(sem("xT_mm"), 1)
            for c in range(KC):
                ins = tr(PS[:, 5, KW * c:KW * c + KW], dw_rows[:, P * c:P * c + P])
            ins.then_inc(sem("dw_mm"), 1)
            for c in range(KC):
                ins = tr(PS[:, 6, HALO * c:HALO * c + HALO], st_rows[:, P * c:P * c + P])
            ins.then_inc(sem("state_mm"), 1)
            pe.wait_ge(sem("ck_in"), 16)
            for h in range(2):
                if h:
                    pe.wait_ge(sem("par_ready"), 1)
                for c in range(4):
                    ins = tr(PS[:, 7 - 3 * h, P * c:P * c + P], ck_tok[:, P * (4 * h + c):P * (4 * h + c) + P])
                ins.then_inc(sem("ck_mm"), 1)
            pe.wait_ge(sem("xT_ready"), KC)

            def channels(s, wait_bank):
                for t in range(4):
                    wait_bank(t)
                    for c in range(KC):
                        ins = pe.matmul(PS[:, t, 0:T], ring[s][:, c, P * t:P * t + P], xT[:, c, :],
                                        start=(c == 0), stop=(c == KC - 1))
                    ins.then_inc(sem("proj_mm"), 1)

            def proj(i):
                for s in range(2):
                    pe.wait_ge(sem(f"ring{s}"), i * 16 + 16)
                    channels(s, lambda t: pe.wait_ge(sem("proj_evac"), i * 8 + (4 * s + t + 1)))

            with pe.Fori(0, 4) as i:
                proj(i)
            pe.wait_ge(sem("u_ready"), 2 * KC)
            pe.wait_ge(sem("state_ready"), 1)
            pe.wait_ge(sem("ckT_ready"), 2)
            for b in range(4):
                col = (HALO + NP_ - HALO) if b < 2 else (US + NS_ - HALO)
                for c in range(4):
                    ins = tr(PS[0:HALO, 4 + b, P * c:P * c + P], uext[:, 4 * (b % 2) + c, col:col + HALO])
                ins.then_inc(sem("convout_mm"), 1)
            with pe.Fori(4, 6) as i:
                proj(i)
            pe.wait_ge(sem("consts"), 1)
            pe.wait_ge(sem("conv"), KW * KC)
            pe.wait_ge(sem("convout_ready"), 4)
            for c in range(KC):
                ins = pe.matmul(PS[:, 4, 0:CONVN], mean_w, yc[:, c, :], start=(c == 0), stop=(c == KC - 1))
            ins.then_inc(sem("mean_mm"), 1)

            def values(s):
                pe.wait_ge(sem(f"ring{s}"), 16 * 7)
                for tt, (t0, r) in enumerate(TT):
                    bank = [0, 1, 2, 3, 6, 7][3 * s + tt]
                    for c in range(KC):
                        ins = pe.matmul(PS[0:r, bank, :], xT[:, c, t0:t0 + r], ring[s][:, c, :],
                                        start=(c == 0), stop=(c == KC - 1))
                    ins.then_inc(sem("v_mm"), 1)

            pe.wait_ge(sem("proj_evac"), 4 + 48)
            values(0)
            pe.wait_ge(sem("sq_ready"), 1)
            for c in range(KC):
                ins = pe.matmul(PS[:, 5, 0:T], mean_w, sq[:, c, :], start=(c == 0), stop=(c == KC - 1))
            ins.then_inc(sem("var_mm"), 1)
            values(1)

            def scores(j):
                if j >= 1:
                    pe.wait_ge(sem("scores_ready"), j)
                else:
                    pe.wait_ge(sem("v_ready"), 6)
                for h in range(2):
                    q = qpad[h]
                    pe.matmul(PS[:, 0, 256 * h:256 * h + 256], q[:, j, P:2 * P], kT[:, j, 0:2 * P], start=True, stop=True)
                    pe.matmul(PS[:, 1, P * h:P * h + P], q[:, j, 0:P], kT[:, j, 0:P], start=True, stop=True)
                    pe.matmul(PS[0:NS_, 2, 192 * h:192 * h + P], q[:, j, 2 * P:T], ckT[:, j, :], start=True, stop=True)
                    ins = pe.matmul(PS[0:NS_, 2, 192 * h + P:192 * h + 192], q[:, j, 2 * P:T], kT[:, j, 2 * P:T],
                                    start=True, stop=True)
                ins.then_inc(sem("score_mm"), 1)

            def pointwise(j):
                s, t = j // 4, j % 4
                if t == 0:
                    pe.wait_ge(sem(f"ring{s}"), 16 * 8)
                if j >= 2:
                    pe.wait_ge(sem("pw_evac"), j - 1)
                for c in range(KC):
                    ins = pe.matmul(PS[:, 6 + j % 2, 0:T], ring[s][:, c, P * t:P * t + P], zc[:, c, :],
                                    start=(c == 0), stop=(c == KC - 1))
                ins.then_inc(sem("pw_mm"), 1)

            def attend(j):
                pr, pt = probs[j % 2], pT[j % 2]
                pe.wait_ge(sem("probs_ready"), j + 1)
                if j >= 1:
                    pe.wait_ge(sem("pT_ready"), j)
                for h in range(2):
                    for kt in range(2):
                        tr(PS[:, 3, (2 * h + kt) * P:(2 * h + kt) * P + P], pr[:, 256 * h + P * kt:256 * h + P * kt + P])
                    tr(PS[:, 4, P * h:P * h + P], pr[:, 512 + P * h:512 + P * h + P])
                    tr(PS[:, 4, 256 + 64 * h:320 + 64 * h], pr[0:64, 768 + 192 * h:768 + 192 * h + P])
                    ins = tr(PS[0:64, 4, 384 + 64 * h:448 + 64 * h], pr[0:64, 768 + 192 * h + P:768 + 192 * h + 192])
                ins.then_inc(sem("p_mm"), 1)
                pe.wait_ge(sem("pT_ready"), j + 1)
                if j >= 1:
                    pe.wait_ge(sem("o_ready"), j)
                for seg in range(3):
                    for h in range(2):
                        o = PS[64 * h:64 * h + 64, 5, :]
                        d = slice(HD * (2 * j + h), HD * (2 * j + h) + HD)
                        if seg == 0:
                            ins = pe.matmul(o[:, 0:P], vtok[:, 0, d], pt[:, 512 + P * h:512 + P * h + P], start=True, stop=True)
                        elif seg == 1:
                            for kt in range(2):
                                ins = pe.matmul(o[:, P:2 * P], vtok[:, kt, d], pt[:, (2 * h + kt) * P:(2 * h + kt) * P + P],
                                                start=(kt == 0), stop=(kt == 1))
                        else:
                            pe.matmul(o[:, 2 * P:T], cv_tok[:, d], pt[:, 768 + 64 * h:832 + 64 * h], start=True, stop=False)
                            ins = pe.matmul(o[:, 2 * P:T], vtok[0:64, 2, d], pt[0:64, 896 + 64 * h:960 + 64 * h],
                                            start=False, stop=True)
                ins.then_inc(sem("o_mm"), 1)

            pe.wait_ge(sem("z_ready"), KC)
            pe.wait_ge(sem("cv_in"), 16)
            scores(0)
            for j in range(PAIRS):
                pointwise(j)
                if j + 1 < PAIRS:
                    scores(j + 1)
                attend(j)
            pe.wait_ge(sem("o_ready"), PAIRS)
            for t in range(KC):
                s = t // 4
                if t % 4 == 0:
                    pe.wait_ge(sem(f"ring{s}"), 16 * 9)
                if t >= 4:
                    pe.wait_ge(sem("mix_ready"), t - 3)
                for c in range(KC):
                    ins = pe.matmul(PS[:, t % 4, 0:T], ring[s][:, c, P * (t % 4):P * (t % 4) + P], oT[:, c, :],
                                    start=(c == 0), stop=(c == KC - 1))
                ins.then_inc(sem("ao_mm"), 1)
            pe.wait_ge(sem("pw_evac"), PAIRS)
            for b in range(6):
                tt, half = b // 2, b % 2
                t0, r = TT[tt]
                if b >= 4:
                    pe.wait_ge(sem("ktok_ready"), b - 3)
                for c in range(4):
                    ins = tr(PS[0:r, 4 + b % 4, P * c:P * c + P], kT[:, 4 * half + c, t0:t0 + r])
                ins.then_inc(sem("ktok_mm"), 1)
            pe.wait_ge(sem("mix_ready"), KC)
            for s in range(2):
                pe.wait_ge(sem(f"ring{s}"), 16 * 10)
                for tt, (t0, r) in enumerate(TT):
                    if s == 1 and tt == 1:
                        pe.wait_ge(sem("ktok_ready"), 6)
                    for c in range(KC):
                        ins = pe.matmul(PS[0:r, 3 * s + tt, :], mixT[:, c, t0:t0 + r], ring[s][:, c, :],
                                        start=(c == 0), stop=(c == KC - 1))
                    ins.then_inc(sem("out_mm"), 1)
            pe.wait_ge(sem("x1_ready"), 3)
            for c in range(KC):
                for t0, r in TT:
                    ins = tr(PS[:, c, t0:t0 + r], xtok[0:r, t0 // P, P * c:P * c + P])
                ins.then_inc(sem("x1T_mm"), 1)
            pe.wait_ge(sem("x1T_a"), 4)
            pe.wait_ge(sem("x1T_d"), 4)
            pe.wait_ge(sem("wr_in"), 32)
            for tt, (t0, r) in enumerate(TT):
                for c in range(KC):
                    ins = pe.matmul(PS[0:r, 0, E * tt:E * tt + E], yacc[:, c, t0:t0 + r], wr[:, c, :],
                                    start=(c == 0), stop=(c == KC - 1))
            ins.then_inc(sem("logit_mm"), 1)
            pe.wait_ge(sem("tri_ready"), 2)
            pe.wait_ge(sem("chosen_ready"), 1)
            for tt in range(3):
                for s in range(tt + 1):
                    pe.matmul(PS[:, 1, E * tt:E * tt + E], tri if s == tt else ones16, chosen[:, s, :],
                              start=(s == 0), stop=(s == tt))
            for s in range(3):
                ins = pe.matmul(PS[:, 1, 3 * E:4 * E], ones16, chosen[:, s, :], start=(s == 0), stop=(s == 2))
            ins.then_inc(sem("rank_mm"), 1)
            for t0, r in TT:
                ins = tr(PS[0:E, 3, t0:t0 + r], gates[0:r, t0 // P, :])
            ins.then_inc(sem("gT_mm"), 1)
            pe.wait_ge(sem("at_place_ready"), 1)
            for k in range(2):
                ins = pe.matmul(PS[0:1, 2, E * k:E * k + E], cols[:, 1 + k:2 + k], at_place, start=True, stop=True)
            ins.then_inc(sem("order_mm"), 1)
            pe.wait_ge(sem("gT_ready"), 1)
            pe.wait_ge(sem("bdown_in"), 16)
            for c in range(KC):
                if c >= 4:
                    pe.wait_ge(sem("yacc"), c - 3)
                pe.matmul(PS[:, 4 + c % 4, 0:T], bdown_sb[:, P * c:P * c + P], gT, start=True, stop=True)\
                  .then_inc(sem("bias_mm"), 1)

            def gather(need):
                pe.wait_ge(sem("sel_ready"), need)
                for c in range(KC):
                    for tt in range(3):
                        for part in range(3):
                            ins = pe.matmul(PS[:, 2, SLOTS * c:SLOTS * c + SLOTS], xh[:, part, tt, P * c:P * c + P],
                                            sel[:, tt, :], start=(tt == 0 and part == 0), stop=(tt == 2 and part == 2))
                ins.then_inc(sem("gather_done"), 1)

            def gate_or_up(bank, w, which, done, parts):
                s, n = P // parts, D // parts
                for h in range(parts):
                    pe.matmul(PS[s * h:s * h + s, bank, 0:n], bsel[:, 0:s], bparts[:, which, n * h:n * h + n],
                              start=True, stop=False)
                for c in range(KC):
                    if c == 0:
                        pe.wait_ge(sem(w[1] + "_0"), w[2])
                    if c == 4:
                        pe.wait_ge(sem(w[1] + "_1"), w[2])
                    for h in range(parts):
                        ins = pe.matmul(PS[s * h:s * h + s, bank, 0:n], xg[:, c, 0:s], w[0][:, c, n * h:n * h + n],
                                        start=False, stop=(c == KC - 1))
                ins.then_inc(sem(done), 1)

            def combine(base):
                for c in range(KC):
                    pe.wait_ge(sem("yacc"), base + (c + KC - 1))
                    pe.matmul(PS[:, 6 + c % 2, 0:T], ysb[:, P * (c % 4):P * (c % 4) + P], scat[c // 4],
                              start=True, stop=True).then_inc(sem("comb_mm"), 1)

            pe.wait_ge(sem("lo_ready"), 3)
            pe.wait_ge(sem("xh_zero"), 3)
            pe.wait_ge(sem("bparts_ready"), 2)
            gather(2)
            pe.wait_ge(sem("yacc"), KC)
            with pe.Fori(0, E // 2) as q:
                for par in range(2):
                    e = q * 2 + par
                    first = pe.value_load(tbl[0:1, bass.ds(e, 1)], min_val=0, max_val=200)
                    full = pe.value_load(tail[0:1, bass.ds(e, 1)], min_val=0, max_val=200)
                    end = pe.value_load(tbl[0:1, bass.ds(e + 1, 1)], min_val=1, max_val=200)

                    def expert_block(i, parts):
                        pe.wait_ge(sem("bsel_ready"), e + 1)
                        pe.wait_ge(sem("xg_ready"), i + 1)
                        gate_or_up(0, (WG[par], f"wg{par}", q * 16 + 16), 0, "gate_done", parts)
                        gate_or_up(1, (WU[par], f"wu{par}", q * 16 + 16), 1, "up_done", parts)
                        gather(i + 3)
                        pe.wait_ge(sem("h_ready"), i + 1)
                        for c in range(KC // parts):
                            ins = tr(PS[:, 3, P * c:P * c + P], act_h[:, P * c:P * c + P])
                        ins.then_inc(sem("hT_mm"), 1)
                        pe.wait_ge(sem("y_sb"), i + 1)
                        pe.wait_ge(sem("scat_ready"), i + 2)
                        combine(i * KC)
                        apart(pe)
                        pe.wait_ge(sem("sgate_ready"), i + 2)
                        for t0, r in TT:
                            ins = tr(PS[0:P // parts, 4, t0:t0 + r], sgate[0:r, t0 // P, 0:P // parts])
                        ins.then_inc(sem("scat_mm"), 1)
                        pe.wait_ge(sem("hT_ready"), i + 2)
                        if parts == 2:
                            for c in range(KC):
                                if c % 4 == 0:
                                    pe.wait_ge(sem(f"wd_{c // 4}"), e * 16 + 16)
                                for h in range(2):
                                    ins = pe.matmul(PS[64 * h:64 * h + 64, 5, :], hT[:, c % 4, c // 4, :],
                                                    WD[:, c, 512 * h:512 * h + 512], start=(c == 0), stop=(c == KC - 1))
                        else:
                            pe.wait_ge(sem("wd_0"), e * 16 + 16)
                            pe.wait_ge(sem("wd_1"), e * 16 + 16)
                            for c in range(4):
                                for h in range(2):
                                    for k in range(2):
                                        r, ck = 64 * h + SMALL * k, 4 * k + c
                                        ins = pe.matmul(PS[r:r + SMALL, 5, :], hT_small[:, ck % 2, ck // 2, :],
                                                        WD[:, ck, 512 * h:512 * h + 512], start=(c == 0), stop=(c == 3))
                        ins.then_inc(sem("down_done"), 1)

                    with pe.If(first < full):
                        with pe.Fori(first, full) as i:
                            expert_block(i, 2)
                    with pe.If(full < end):
                        with pe.Fori(full, end) as i:
                            expert_block(i, 4)
            total = pe.value_load(tbl[0:1, E:E + 1], min_val=1, max_val=200)
            pe.wait_ge(sem("y_sb"), total + 1)
            pe.wait_ge(sem("scat_ready"), total + 2)
            combine(total * KC)
            pe.wait_ge(sem("yacc"), total * KC + 2 * KC)
            for tt, (t0, r) in enumerate(TT):
                for s in range(2):
                    for c in range(4):
                        ins = tr(PS[0:r, 2 * tt + s, P * c:P * c + P], yacc[:, 4 * s + c, t0:t0 + r])
                    ins.then_inc(sem("y_mm"), 1)


_INS = ["x_prompt", "x_sample", "cache_k", "cache_v", "state_conv", "w_in", "b_in", "rel_bias", "w_att_o",
        "w_dw", "b_dw", "conv_ln_g", "conv_ln_b", "w_pw", "w_out", "b_out", "ln1_g", "ln1_b", "w_router",
        "b_router", "w_gate", "b_gate", "w_up", "b_up", "w_down", "b_down", "ln2_g", "ln2_b"]
_OUTS = [(1, 256, 1024), (1, 64, 1024), (1, 1, 256, 16, 64), (1, 1, 256, 16, 64), (1, 1, 30, 1024),
         (1, 1, 128, 16, 64), (1, 1, 128, 16, 64), (1, 1, 30, 1024)]


def kernel(**inputs):
    import numpy as _np
    import concourse.bacc as _bacc
    from concourse import mybir as _mybir
    from concourse.bass_utils import run_bass_kernel_spmd as _run

    nc = _bacc.Bacc("TRN2", target_bir_lowering=False, num_devices=1)
    arrays, args = {}, []
    for name in _INS:
        a = _np.ascontiguousarray(inputs[name])
        arrays[f"in_{name}_dram"] = a
        args.append(nc.dram_tensor(f"in_{name}_dram", a.shape, _mybir.dt.from_np(a.dtype), kind="ExternalInput").ap())
    for i, shape in enumerate(_OUTS):
        args.append(nc.dram_tensor(f"out_{i}_dram", shape, _mybir.dt.float32, kind="ExternalOutput").ap())
    encoder_step(nc, *args)
    r = _run(nc, [arrays], core_ids=[0])
    return tuple(r.results[0][f"out_{i}_dram"] for i in range(len(_OUTS)))
```

```python
from contextlib import ExitStack

import concourse.bass as bass
from concourse import mybir

ALU = mybir.AluOpType
ACT = mybir.ActivationFunctionType
AXX = mybir.AxisListType.X
F32 = mybir.dt.float32
BF16 = mybir.dt.bfloat16
F16 = mybir.dt.float16
I32 = mybir.dt.int32
U32 = mybir.dt.uint32

P = 128
D = 1024
KC = D // P
NP_, NS_ = 256, 64
T = NP_ + NS_
TT = [(0, 128), (128, 128), (256, 64)]
H, HD = 16, 64
PAIRS = H // 2
PAST = 128
KW = 31
HALO = KW - 1
UEXT = 384
US = HALO + NP_ + HALO
CONVN = NP_ + HALO + NS_
E = 32
TOPK = 4
SLOTS = 64
SMALL = 32
MAXREL = 128
NREL = 2 * MAXREL + 1
REV = 384
ALPHA = 2.0 ** 0.25
EPS = 1e-5
LIMIT = 7.0
SW_ALPHA = 1.702
SCALE = HD ** -0.5
NEG = -1e30


def encoder_step(nc, x_prompt, x_sample, cache_k, cache_v, state_conv, w_in, b_in, rel_bias, w_att_o,
                 w_dw, b_dw, conv_ln_g, conv_ln_b, w_pw, w_out, b_out, ln1_g, ln1_b, w_router, b_router,
                 w_gate, b_gate, w_up, b_up, w_down, b_down, ln2_g, ln2_b,
                 y_prompt, y_sample, new_k_p, new_v_p, new_conv_p, new_k_s, new_v_s, new_conv_s):
    BROW = H * REV
    rev_dram = nc.dram_tensor("rev_bias", [P, BROW + 1], F32, kind="Internal").ap()

    def rows(ap):
        return ap[0].rearrange("(c p) n -> p c n", p=P)

    w_in_v = rows(w_in).rearrange("p c (b s n) -> p c b s n", s=2, n=512)
    w_pw_v, w_att_v, w_out_v = (rows(w).rearrange("p c (s n) -> p c s n", s=2) for w in (w_pw, w_att_o, w_out))
    wg_v, wu_v, wd_v = (w[0].rearrange("e (c p) n -> e p c n", p=P) for w in (w_gate, w_up, w_down))
    ck_v = cache_k[0, 0].rearrange("t h d -> t (h d)")
    cv_v = cache_v[0, 0].rearrange("t h d -> t (h d)")
    nks_v = new_k_s[0, 0].rearrange("t h d -> t (h d)")
    nvs_v = new_v_s[0, 0].rearrange("t h d -> t (h d)")
    nkp_v = new_k_p[0, 0].rearrange("(t p) h d -> p t (h d)", p=P)
    nvp_v = new_v_p[0, 0].rearrange("(t p) h d -> p t (h d)", p=P)

    ctx = ExitStack()
    with ctx:
        WB = KC * D
        ZONE = 5 * WB
        SB = ctx.enter_context(nc.sbuf_tensor("SB", [P, ZONE + 12200], F32))
        PS = ctx.enter_context(nc.psum_tensor("PS", [P, 8, 512], F32))

        def view(off, *dims, rows=P):
            n = 1
            for d in dims:
                n *= d
            ap = SB[0:rows, off:off + n]
            if len(dims) == 2:
                ap = ap.rearrange("p (a b) -> p a b", a=dims[0])
            if len(dims) == 3:
                ap = ap.rearrange("p (a b c) -> p a b c", a=dims[0], b=dims[1])
            return ap

        def view16(off, dt, *dims, rows=P):
            n = 1
            for d in dims:
                n *= d
            ap = SB[0:rows, off:off + (n + 1) // 2].bitcast(dt)
            if len(dims) == 2:
                ap = ap.rearrange("p (a b) -> p a b", a=dims[0])
            if len(dims) == 3:
                ap = ap.rearrange("p (a b c) -> p a b c", a=dims[0], b=dims[1])
            return ap

        wbuf = [view(i * WB, KC, D) for i in range(5)]
        WG, WU, WD = (wbuf[0], wbuf[3]), (wbuf[1], wbuf[4]), wbuf[2]
        ring = [view(s * 4096, KC, 512) for s in range(2)]
        qpad = [view(WB + h * 2560, KC, T) for h in range(2)]
        kT = view(WB + 5120, KC, T)
        parT = view(WB + 7680, 80)
        dwT = view(WB + 7760, KC, KW)
        mean_w = view(WB + 8008, P)
        yc = view(2 * WB, KC, CONVN)
        sq = view(2 * WB, KC, T)
        rstd_c = view(2 * WB + 2800, T)
        relb = view(2 * WB, H, 2 * P)
        bv_bc = view(2 * WB + 4096, D)
        probs = [view(2 * WB + 4096 + i * 1152, 1152) for i in range(2)]
        ck_tok = view(2 * WB + 6400, D)
        xtok = view(3 * WB, 3, D)
        vtok = view(3 * WB + 3072, 3, D)
        cv_tok = view(3 * WB + 6144, D)
        ckT = view(3 * WB + 7168, KC, P)
        wr = view(3 * WB + 6800, KC, E)
        br_bc = view(3 * WB + 7100, E)
        ua = view(4 * WB, KC, T)
        zc = ua
        ga = view(4 * WB + 2560, KC, T)
        gb = view(4 * WB + 5120, KC, T)
        braw = view(4 * WB + 2560, 2, D, rows=96)
        xT = view(ZONE, KC, T)
        mixT = xT
        ub = view(ZONE + 2560, KC, T)
        oT = ub
        uext = view(ZONE + 5120, KC, UEXT)
        ktok = view(ZONE + 5120, 3, D)
        bout_bc = view(ZONE + 8192, D)
        convout = view(ZONE + 8192, 2, D, rows=HALO)
        pT = [view(ZONE + 8192 + i * 1024, 1024) for i in range(2)]
        ln1g_bc, ln1b_bc = pT
        gT = SB[P - E:P, ZONE + 8192:ZONE + 8192 + T]
        xh = view16(ZONE, BF16, 3, 3, D)
        yacc = view(ZONE + 4608, KC, T)
        xg = view(ZONE + 7168, KC, SLOTS)
        gmin = view(ZONE + 7680, 512)
        hT = view(ZONE + 7680, 4, 2, SLOTS)
        hT_small = view(ZONE + 7680, 2, 4, SMALL)
        act_h = view(ZONE + 8192, 512)
        ysb = view(ZONE + 8704, 512)
        scat = [view(ZONE + 9216 + h * T, T) for h in range(2)]
        sgate = view(ZONE + 9856, 3, SLOTS)
        sel = view16(ZONE + 10048, BF16, 3, SLOTS)
        bsel = [view16(o, BF16, SLOTS, rows=96) for o in (ZONE + 10144, ZONE + 12168)]
        K0 = ZONE + 10240
        bparts = view16(K0, BF16, 2, D, rows=96)
        bdown_sb = SB[P - E:P, K0:K0 + D]
        ident = view(K0 + 1024, P)
        iota = view16(K0 + 1152, F16, T)
        onehot = view16(K0 + 1312, BF16, E, rows=96)
        eps_c = view(K0 + 1328, 1)
        tbl = view(K0 + 1330, 34, rows=1).bitcast(I32)
        gates = view(K0 + 1364, 3, E)
        rank = view(K0 + 1460, 3, E)
        sm = K0 + 1556
        stats = view(sm, 3, 12)
        mv = view(sm + 36, 3, 2)
        rstd = view(sm + 42, 3)
        nmax = view(sm + 48, 12)
        psumr = view(sm + 60, 12)
        rsum = view(sm + 72, 12)
        nblk = view(sm + 84, E, rows=1).bitcast(I32)
        dist = view(sm + 116, 3, SLOTS)
        tail = view(sm + 308, E, rows=1).bitcast(I32)
        order = view(sm + 340, E, rows=1).bitcast(I32)
        R0 = ZONE + 7168
        lg = view(R0, 3, E)
        top8 = view(R0 + 96, 3, 8)
        idx8 = view(R0 + 120, 3, 8).bitcast(U32)
        idxf = view(R0 + 144, 3 * TOPK)
        e4 = view(R0 + 168, 3, 4)
        ssum = view(R0 + 180, 3)
        rs4 = view(R0 + 184, 3)
        ntop = view(R0 + 188, 3)
        term = view(R0 + 192, 3, TOPK, E)
        chosen = view16(R0 + 576, BF16, 3, E)
        tri = view16(R0 + 624, BF16, P)
        ones16 = view16(R0 + 688, BF16, P)
        cnt = view(R0 + 752, E, rows=1)
        nb = view(R0 + 784, E, rows=1)
        cum = view(R0 + 816, E, rows=1)
        one_r = view(R0 + 848, E, rows=1)
        small = view(R0 + 880, E, rows=1)
        R1 = 3 * WB + 6500
        key = view(R1, E, rows=E)
        diag = view(R1 + 32, 3, E, rows=E)
        cols = view(R1 + 128, 3, rows=E)
        above = view(R1 + 132, 1, rows=E)
        at_place = view(R1 + 136, E, rows=E)
        tie = view(R1 + 168, E, rows=E)
        above_at = view(R1 + 200, E, rows=E)
        par_rows = view(ZONE + 2560, P, rows=80)
        dw_rows = view(ZONE + 2560 + P, D, rows=KW)
        st_rows = view(ZONE + 2560 + P + D, D, rows=HALO)
        rb_sb = view(2 * WB, NREL, rows=H)
        rev_sb = view(2 * WB + NREL, REV, rows=H)

        def psv(bank, n, a=None):
            ap = PS[:, bank, 0:n]
            return ap

        sems = {}

        def sem(name):
            if name not in sems:
                sems[name] = ctx.enter_context(nc.semaphore(name))
            return sems[name]

        def apart(eng):
            eng.wait_ge(sem("tables_done"), 1)

        COMB_BANK = [6, 7, 1, 6, 7, 1, 6, 7]

        def load_by(eng, buf, src, name, used=None, count=None):
            for h in range(2):
                if used is not None:
                    eng.wait_ge(sem(used[h]), count)
                eng.dma_start(buf[:, 4 * h:4 * h + 4, :], src[:, 4 * h:4 * h + 4, :]).then_inc(sem(f"{name}_{h}"), 16)

        def weights(v, e):
            return v[bass.ds(e, 1)].rearrange("a p c n -> p (a c) n")

        block = ctx.enter_context(nc.Block())

        @block.sync
        def _(sp):
            sp.dma_start(xtok[:, 0:2, :], x_prompt[0].rearrange("(t p) n -> p t n", p=P)).then_inc(sem("x_in"), 16)
            sp.dma_start(xtok[0:NS_, 2, :], x_sample[0]).then_inc(sem("x_in"), 16)
            sp.dma_start(par_rows[0:56, :], b_in.rearrange("a (c p) -> (a c) p", p=P)).then_inc(sem("par_in"), 16)
            sp.dma_start(par_rows[56:64, :], b_dw.rearrange("a (c p) -> (a c) p", p=P)).then_inc(sem("par_in"), 16)
            sp.dma_start(par_rows[64:72, :], conv_ln_g.rearrange("a (c p) -> (a c) p", p=P)).then_inc(sem("par_in"), 16)
            sp.dma_start(par_rows[72:80, :], conv_ln_b.rearrange("a (c p) -> (a c) p", p=P)).then_inc(sem("par_in"), 16)
            sp.dma_start(dw_rows, w_dw[0]).then_inc(sem("par_in"), 16)
            sp.dma_start(st_rows, state_conv[0, 0]).then_inc(sem("par_in"), 16)
            for s in range(2):
                sp.dma_start(ring[s], w_in_v[:, :, 3, s, :]).then_inc(sem(f"ring{s}"), 16)
            sp.dma_start(ck_tok, ck_v).then_inc(sem("ck_in"), 16)
            sp.dma_start(cv_tok, cv_v).then_inc(sem("cv_in"), 16)
            sp.dma_start(bv_bc, b_in[:, 2 * D:3 * D].broadcast_to([P, D])).then_inc(sem("bv_in"), 16)
            sp.dma_start(bout_bc, b_out.broadcast_to([P, D])).then_inc(sem("bout_in"), 16)
            sp.dma_start(rb_sb, rel_bias[0]).then_inc(sem("rb_in"), 16)
            for g in range(3):
                sp.dma_start(braw[32 * g:32 * g + 32, 0, :], b_gate[0]).then_inc(sem("braw_in"), 16)
                sp.dma_start(braw[32 * g:32 * g + 32, 1, :], b_up[0]).then_inc(sem("braw_in"), 16)
            sp.dma_start(bdown_sb, b_down[0]).then_inc(sem("bdown_in"), 16)
            sp.wait_ge(sem("rev_done"), 1)
            sp.dma_start(bass.AP(tensor=rev_dram.tensor, offset=0, ap=[[REV, H], [BROW + 1, P], [1, REV]]),
                         rev_sb.rearrange("h (a n) -> h a n", a=1).broadcast_to([H, P, REV])).then_inc(sem("rev_out"), 16)

            def group(s, src, user, count):
                sp.wait_ge(sem(user), count)
                sp.dma_start(ring[s], src).then_inc(sem(f"ring{s}"), 16)

            with sp.Fori(1, 4) as i:
                for s in range(2):
                    group(s, w_in_v[:, :, bass.ds(i + 3, 1), s, :].rearrange("p c a n -> p c (a n)"), "proj_mm", i * 8 + (4 * s - 4))
            with sp.Fori(4, 6) as i:
                for s in range(2):
                    group(s, w_in_v[:, :, bass.ds(i - 4, 1), s, :].rearrange("p c a n -> p c (a n)"), "proj_mm", i * 8 + (4 * s - 4))
            for s in range(2):
                group(s, w_in_v[:, :, 2, s, :], "proj_mm", 44 + 4 * s)
            sp.wait_ge(sem("rev_out"), 16)
            sp.wait_ge(sem("z_ready"), KC)
            src = bass.AP(tensor=rev_dram.tensor, offset=P - 1, ap=[[BROW, P], [REV, H], [1, 2 * P]])
            sp.dma_start(relb, src).then_inc(sem("relb_in"), 16)
            for s in range(2):
                group(s, w_pw_v[:, :, s, :], "v_mm", 3 * (s + 1))
            for s in range(2):
                group(s, w_att_v[:, :, s, :], "pw_mm", 4 * (s + 1))
            def load(buf, src, name):
                load_by(sp, buf, src, name)

            sp.wait_ge(sem("p_mm"), PAIRS)
            load(WD, wd_v[0], "wd")
            sp.wait_ge(sem("o_mm"), PAIRS)
            sp.dma_start(ln1g_bc, ln1_g.broadcast_to([P, D])).then_inc(sem("ln1_in"), 16)
            sp.dma_start(ln1b_bc, ln1_b.broadcast_to([P, D])).then_inc(sem("ln1_in"), 16)
            sp.dma_start(wr, rows(w_router)).then_inc(sem("wr_in"), 16)
            sp.dma_start(br_bc, b_router.broadcast_to([P, E])).then_inc(sem("wr_in"), 16)
            for s in range(2):
                group(s, w_out_v[:, :, s, :], "ao_mm", 4 * (s + 1))
            sp.wait_ge(sem("ktok_mm"), 6)
            load(WU[0], wu_v[0], "wu0")
            sp.wait_ge(sem("mix_ready"), KC)
            load(WU[1], wu_v[1], "wu1")
            sp.wait_ge(sem("out_mm"), 6)
            load(WG[0], wg_v[0], "wg0")
            sp.wait_ge(sem("lo_ready"), 3)
            sp.wait_ge(sem("tables_done"), 1)
            sp.wait_ge(sem("v_out"), 32)
            load(WG[1], wg_v[1], "wg1")

            def expert_at(place):
                return sp.value_load(order[0:1, bass.ds(place, 1)], min_val=0, max_val=E - 1)

            with sp.Fori(1, E // 2) as q:
                for par in range(2):
                    first = sp.value_load(tbl[0:1, bass.ds(q * 2 + (par - 1), 1)], min_val=1, max_val=200)
                    blocks = sp.value_load(nblk[0:1, bass.ds(q * 2 + (par - 2), 1)], min_val=1, max_val=T // SLOTS)
                    e, e_before = expert_at(q * 2 + par), expert_at(q * 2 + (par - 1))

                    def load_up():
                        load_by(sp, WU[par], weights(wu_v, e), f"wu{par}", ["up_half", "up_done"], first + 1)

                    def load_down():
                        load_by(sp, WD, weights(wd_v, e_before), "wd", ["down_half", "down_done"], first)

                    load_by(sp, WG[par], weights(wg_v, e), f"wg{par}", ["gate_half", "gate_done"], first)
                    with sp.If(blocks > 1):
                        load_up()
                        load_down()
                    with sp.If(blocks < 2):
                        load_down()
                        load_up()
            last = sp.value_load(tbl[0:1, E - 1:E], min_val=1, max_val=200)
            e = sp.value_load(order[0:1, E - 1:E], min_val=0, max_val=E - 1)
            load_by(sp, WD, weights(wd_v, e), "wd", ["down_half", "down_done"], last)
            sp.wait_ge(sem("up_done"), last + 1)
            sp.dma_start(WG[0][:, 0, :], ln2_g.broadcast_to([P, D])).then_inc(sem("ln2_in"), 16)
            sp.dma_start(WG[0][:, 1, :], ln2_b.broadcast_to([P, D])).then_inc(sem("ln2_in"), 16)
            for tt in range(2):
                sp.wait_ge(sem("y_ready"), tt + 1)
                sp.dma_start(y_prompt[0, P * tt:P * tt + P, :], WG[0][:, 2 + tt, :]).then_inc(sem("y_out"), 16)
            sp.wait_ge(sem("y_ready"), 3)
            sp.dma_start(y_sample[0], WG[0][0:NS_, 4, :]).then_inc(sem("y_out"), 16)
            sp.wait_ge(sem("y_out"), 48)

        @block.gpsimd
        def _(pool):
            n = [0]

            def link(ins):
                n[0] += 1
                ins.then_inc(sem("pool_chain"), 1)
                pool.wait_ge(sem("pool_chain"), n[0])

            pool.sem_inc(sem("proj_evac"), 4)
            for name in ("sel_ready", "sgate_ready", "gather_done", "scat_mm", "up_half", "up_done", "hT_ready"):
                pool.sem_inc(sem(name), 1)
            link(pool.memset(ident, 0.0))
            pool.affine_select(ident, ident, pattern=[[-1, P]], compare_op=ALU.not_equal, fill=1.0,
                               base=0, channel_multiplier=1).then_inc(sem("ident_ready"), 1)
            pool.memset(mean_w, 1.0 / D).then_inc(sem("consts"), 1)
            pool.memset(eps_c, EPS).then_inc(sem("consts"), 1)
            pool.memset(uext[:, :, 0:HALO], 0.0).then_inc(sem("uext_zero"), 1)
            pool.wait_ge(sem("uext_zero"), 1)
            pool.memset(qpad[0][64:128], 0.0).then_inc(sem("qpad_zero"), 1)
            pool.wait_ge(sem("qpad_zero"), 1)
            pool.memset(qpad[1][0:64], 0.0).then_inc(sem("qpad_zero"), 1)
            pool.wait_ge(sem("qpad_zero"), 2)
            pool.iota(iota, [[1, T]], base=0, channel_multiplier=0,
                      allow_small_or_imprecise_dtypes=True).then_inc(sem("iota_ready"), 1)
            pool.wait_ge(sem("ident_ready"), 1)
            pool.wait_ge(sem("iota_ready"), 1)
            for g in range(3):
                s = slice(32 * g, 32 * g + 32)
                pool.tensor_copy(onehot[s, :], ident[s, s]).then_inc(sem("onehot_ready"), 1)
                pool.wait_ge(sem("onehot_ready"), g + 1)
            pool.wait_ge(sem("xT_mm"), KC)
            pool.wait_ge(sem("bout_in"), 16)
            for tt, (_, r) in enumerate(TT):
                link(pool.tensor_scalar(xtok[0:r, tt, :], xtok[0:r, tt, :], ALPHA, None, ALU.mult))
                pool.tensor_tensor(xtok[0:r, tt, :], xtok[0:r, tt, :], bout_bc[0:r], ALU.add).then_inc(sem("xr_ready"), 1)
                pool.wait_ge(sem("xr_ready"), tt + 1)
            pool.wait_ge(sem("braw_in"), 96)
            link(pool.tensor_copy(bparts, braw))
            link(pool.tensor_tensor(braw, braw, bparts, ALU.subtract))
            pool.tensor_copy(bparts[32:64], braw[32:64]).then_inc(sem("bparts_ready"), 1)
            pool.wait_ge(sem("bparts_ready"), 1)
            link(pool.tensor_copy(bparts[64:96], braw[64:96]))
            link(pool.tensor_tensor(braw[64:96], braw[64:96], bparts[64:96], ALU.subtract))
            pool.tensor_copy(bparts[64:96], braw[64:96]).then_inc(sem("bparts_ready"), 1)
            pool.dma_start(nks_v[0:PAST - NS_], ck_v[NS_:PAST]).then_inc(sem("kv_out"), 16)
            pool.dma_start(nvs_v[0:PAST - NS_], cv_v[NS_:PAST]).then_inc(sem("kv_out"), 16)
            pool.wait_ge(sem("convout_ready"), 4)
            pool.dma_start(new_conv_p[0, 0], convout[:, 0, :]).then_inc(sem("conv_out"), 16)
            pool.dma_start(new_conv_s[0, 0], convout[:, 1, :]).then_inc(sem("conv_out"), 16)
            pool.wait_ge(sem("v_ready"), 6)
            pool.dma_start(nvp_v, vtok[:, 0:2, :]).then_inc(sem("v_out"), 16)
            pool.dma_start(nvs_v[PAST - NS_:PAST], vtok[0:NS_, 2, :]).then_inc(sem("v_out"), 16)
            pool.wait_ge(sem("ktok_ready"), 6)
            pool.dma_start(nkp_v, ktok[:, 0:2, :]).then_inc(sem("k_out"), 16)
            pool.dma_start(nks_v[PAST - NS_:PAST], ktok[0:NS_, 2, :]).then_inc(sem("k_out"), 16)
            pool.wait_ge(sem("k_out"), 32)
            link(pool.memset(tri, 1.0))
            pool.affine_select(tri, tri, pattern=[[1, P]], compare_op=ALU.is_ge, fill=0.0,
                               base=0, channel_multiplier=-1).then_inc(sem("tri_ready"), 1)
            pool.memset(ones16, 1.0).then_inc(sem("tri_ready"), 1)
            pool.wait_ge(sem("tri_ready"), 2)
            def remainder(out, a, b, tt, ready, done):
                r = TT[tt][1]
                pool.wait_ge(sem(ready), tt + 1)
                pool.tensor_tensor(out[0:r], a[0:r], b[0:r], ALU.subtract).then_inc(sem(done), 1)
                pool.wait_ge(sem(done), tt + 1)

            for tt in range(3):
                pool.wait_ge(sem("x1T_mm"), KC if tt < 2 else 2 * KC)
                remainder(xtok[:, tt, :], xtok[:, tt, :], xh[:, 0, tt, :], tt, "hi_ready", "resid1")
                remainder(xh[:, 2, tt, :], xtok[:, tt, :], xh[:, 1, tt, :], tt, "mid_ready", "lo_ready")
            pool.wait_ge(sem("tables_done"), 1)
            pool.wait_ge(sem("onehot_ready"), 3)

            with pool.Fori(0, E // 2) as q:
                for par in range(2):
                    k = q * 2 + par
                    first = pool.value_load(tbl[0:1, bass.ds(k, 1)], min_val=0, max_val=200)
                    blocks = pool.value_load(nblk[0:1, bass.ds(k, 1)], min_val=1, max_val=T // SLOTS)
                    e = pool.value_load(order[0:1, bass.ds(k, 1)], min_val=0, max_val=E - 1)
                    apart(pool)
                    pool.wait_ge(sem("gather_done"), first + 1)
                    pool.wait_ge(sem("sgate_ready"), first + 1)
                    pool.tensor_copy(bsel[par], onehot[:, bass.ds(e, 1)].broadcast_to([96, SLOTS])).then_inc(sem("bsel_ready"), 1)
                    with pool.Fori(0, blocks) as b:
                        i = first + b
                        apart(pool)
                        pool.wait_ge(sem("bsel_ready"), k + 1)
                        pool.wait_ge(sem("sel_ready"), i + 1)
                        pool.tensor_tensor(dist, iota[:, bass.ds(b * SLOTS, SLOTS)].rearrange("p (a s) -> p a s", a=1).broadcast_to([P, 3, SLOTS]),
                                           rank[:, :, bass.ds(e, 1)].broadcast_to([P, 3, SLOTS]),
                                           ALU.subtract).then_inc(sem("dist_ready"), 1)
                        apart(pool)
                        pool.wait_ge(sem("dist_ready"), i + 1)
                        pool.wait_ge(sem("gather_done"), i + 1)
                        pool.tensor_scalar(sel, dist, 0.0, None, ALU.is_equal).then_inc(sem("sel_ready"), 1)
                        pool.wait_ge(sem("scat_mm"), i + 1)
                        pool.wait_ge(sem("sel_ready"), i + 2)
                        pool.tensor_tensor(sgate, sel, gates[:, :, bass.ds(e, 1)].broadcast_to([P, 3, SLOTS]),
                                           ALU.mult).then_inc(sem("sgate_ready"), 1)
            total = pool.value_load(tbl[0:1, E:E + 1], min_val=1, max_val=200)
            pool.wait_ge(sem("gather_done"), total + 1)
            pool.tensor_tensor(sel, sel, sel, ALU.subtract).then_inc(sem("sel_ready"), 1)
            pool.wait_ge(sem("kv_out"), 32)
            pool.wait_ge(sem("conv_out"), 32)
            pool.wait_ge(sem("v_out"), 32)

        @block.scalar
        def _(act):
            act.wait_ge(sem("par_ready"), 1)
            def tile(i, s, t, dst, func, col):
                act.wait_ge(sem("proj_mm"), i * 8 + (s * 4 + t + 1))
                c = s * 4 + t
                act.activation(dst[:, bass.ds(c, 1), :].rearrange("p a n -> p (a n)"), PS[:, t, 0:T], func,
                               bias=parT[:, bass.ds(col + c, 1)]).then_inc(sem("proj_evac"), 1)

            for i, (dst, func, col) in enumerate([(ua, ACT.Identity, 24), (ub, ACT.Sigmoid, 32),
                                                  (ga, ACT.Sigmoid, 40), (gb, ACT.Sigmoid, 48)]):
                if i == 2:
                    act.wait_ge(sem("bparts_ready"), 2)
                with act.Fori(0, 2) as s:
                    for t in range(4):
                        tile(i, s, t, dst, func, col)
            for h in range(2):
                act.wait_ge(sem("ck_mm"), h + 1)
                act.copy(ckT[:, 4 * h:4 * h + 4, :], PS[:, 7 - 3 * h, :].rearrange("p (c k) -> p c k", c=4))\
                   .then_inc(sem("ckT_ready"), 1)
            for b in range(4):
                act.wait_ge(sem("convout_mm"), b + 1)
                if b == 0:
                    act.wait_ge(sem("xr_ready"), 3)
                act.copy(convout[:, b // 2, (b % 2) * 512:(b % 2) * 512 + 512],
                         PS[0:HALO, 4 + b, 0:512]).then_inc(sem("convout_ready"), 1)
            act.wait_ge(sem("qpad_zero"), 2)
            with act.Fori(0, 2) as s:
                for t in range(4):
                    act.wait_ge(sem("proj_mm"), s * 4 + (32 + t + 1))
                    for h in range(2):
                        r = slice(64 * h, 64 * h + 64)
                        ins = act.activation(qpad[h][r, bass.ds(s * 4 + t, 1), :].rearrange("p a n -> p (a n)"), PS[r, t, 0:T],
                                             ACT.Identity, bias=parT[r, bass.ds(s * 4 + t, 1)])
                    ins.then_inc(sem("proj_evac"), 1)
            with act.Fori(0, 2) as s:
                for t in range(4):
                    tile(5, s, t, kT, ACT.Identity, 8)
            act.wait_ge(sem("zc_centred"), 2)
            act.activation(sq, zc, ACT.Square).then_inc(sem("sq_ready"), 1)
            act.wait_ge(sem("var_mm"), 1)
            act.wait_ge(sem("consts"), 2)
            act.activation(rstd_c, PS[:, 5, 0:T], ACT.Sqrt, bias=eps_c).then_inc(sem("std_c"), 1)
            act.wait_ge(sem("z_norm"), 1)
            for c in range(KC):
                act.activation(zc[:, c, :], zc[:, c, :], ACT.Silu, bias=parT[:, 72 + c:73 + c],
                               scale=parT[:, 64 + c:65 + c]).then_inc(sem("z_ready"), 1)

            def exps(j):
                pr = probs[j % 2]
                act.wait_ge(sem("scores_ready"), j + 1)
                k = 6 * (j % 2)
                for a, (o, w, r) in enumerate([(0, 256, 128), (256, 256, 128), (512, 128, 128), (640, 128, 128),
                                               (768, 192, 64), (960, 192, 64)]):
                    ins = act.activation(pr[0:r, o:o + w], pr[0:r, o:o + w], ACT.Exp, bias=nmax[0:r, k + a:k + a + 1],
                                         accum_out=psumr[0:r, k + a:k + a + 1])
                ins.then_inc(sem("exp_done"), 1)

            def evac_p(j):
                pt = pT[j % 2]
                act.wait_ge(sem("p_mm"), j + 1)
                if j == 0:
                    act.wait_ge(sem("conv_out"), 32)
                act.copy(pt[:, 0:512], PS[:, 3, :])
                act.copy(pt[:, 512:896], PS[:, 4, 0:384])
                act.copy(pt[0:64, 896:1024], PS[0:64, 4, 384:512]).then_inc(sem("pT_ready"), 1)

            def evac_o(j):
                act.wait_ge(sem("o_mm"), j + 1)
                act.copy(oT[:, j, :], PS[:, 5, 0:T]).then_inc(sem("o_ready"), 1)

            for j in range(PAIRS):
                exps(j)
                if j >= 1:
                    evac_o(j - 1)
                evac_p(j)
            evac_o(PAIRS - 1)
            for b in range(6):
                tt, half = b // 2, b % 2
                r = TT[tt][1]
                act.wait_ge(sem("ktok_mm"), b + 1)
                act.copy(ktok[0:r, tt, half * 512:half * 512 + 512], PS[0:r, 4 + b % 4, :]).then_inc(sem("ktok_ready"), 1)
            def std1(tt):
                r = TT[tt][1]
                act.wait_ge(sem("var1"), tt + 1)
                act.activation(rstd[0:r, tt:tt + 1], mv[0:r, tt, 1:2], ACT.Sqrt, bias=eps_c[0:r]).then_inc(sem("std1"), 1)

            std1(0)
            act.wait_ge(sem("k_out"), 32)

            def high(tt):
                r = TT[tt][1]
                act.wait_ge(sem("x1_ready"), tt + 1)
                act.copy(xh[0:r, 0, tt, :], xtok[0:r, tt, :]).then_inc(sem("hi_ready"), 1)

            def middle(tt):
                r = TT[tt][1]
                act.wait_ge(sem("resid1"), tt + 1)
                act.copy(xh[0:r, 1, tt, :], xtok[0:r, tt, :]).then_inc(sem("mid_ready"), 1)

            std1(1)
            std1(2)
            for c in range(KC):
                act.wait_ge(sem("x1T_mm"), c + 1)
                act.copy(yacc[:, c, 0:NP_], PS[:, c, 0:NP_]).then_inc(sem("x1T_a"), 1)
            for tt in range(3):
                high(tt)
            middle(0)
            act.wait_ge(sem("top_ready"), 1)
            for tt in range(3):
                act.activation(e4[:, tt, :], top8[:, tt, 0:4], ACT.Exp, bias=ntop[:, tt:tt + 1],
                               accum_out=ssum[:, tt:tt + 1]).then_inc(sem("e4_ready"), 1)
            middle(1)
            middle(2)
            act.wait_ge(sem("gT_mm"), 1)
            act.copy(gT, PS[0:E, 3, 0:T]).then_inc(sem("gT_ready"), 1)

            act.wait_ge(sem("tables_done"), 1)
            act.wait_ge(sem("gather_done"), 2)
            act.copy(xg, PS[:, 2, :].rearrange("p (c s) -> p c s", c=KC)).then_inc(sem("xg_ready"), 1)

            def expert_block(i, n):
                act.wait_ge(sem("gmin_ready"), i + 1)
                act.activation(act_h[:, 0:n], gmin[:, 0:n], ACT.Sigmoid, scale=SW_ALPHA).then_inc(sem("sig_ready"), 1)
                act.wait_ge(sem("gather_done"), i + 3)
                act.copy(xg, PS[:, 2, :].rearrange("p (c s) -> p c s", c=KC)).then_inc(sem("xg_ready"), 1)
                act.wait_ge(sem("hT_mm"), i + 1)
                if n == 512:
                    act.copy(hT, PS[:, 3, :].rearrange("p (c h s) -> p c h s", c=4, h=2)).then_inc(sem("hT_ready"), 1)
                else:
                    act.copy(hT_small, PS[:, 3, 0:256].rearrange("p (c h s) -> p c h s", c=2, h=4)).then_inc(sem("hT_ready"), 1)
                act.wait_ge(sem("down_done"), i + 1)
                act.copy(ysb, PS[:, 5, :]).then_inc(sem("y_sb"), 1)

            with act.Fori(0, E) as k:
                first = act.value_load(tbl[0:1, bass.ds(k, 1)], min_val=0, max_val=200)
                full = act.value_load(tail[0:1, bass.ds(k, 1)], min_val=0, max_val=200)
                end = act.value_load(tbl[0:1, bass.ds(k + 1, 1)], min_val=1, max_val=200)
                with act.If(first < full):
                    with act.Fori(first, full) as i:
                        expert_block(i, 512)
                with act.If(full < end):
                    with act.Fori(full, end) as i:
                        expert_block(i, 256)
            act.wait_ge(sem("var2"), 1)
            act.activation(rstd, mv[:, :, 1], ACT.Sqrt, bias=eps_c).then_inc(sem("std2"), 1)
            act.wait_ge(sem("shift2"), 1)
            for tt, (_, r) in enumerate(TT):
                act.activation(WG[0][0:r, 2 + tt, :].rearrange("p (s n) -> p s n", s=2), PS[0:r, 2 * tt:2 * tt + 2, :],
                               ACT.Identity, bias=nmax[0:r, tt:tt + 1], scale=rstd[0:r, tt:tt + 1]).then_inc(sem("norm2"), 1)

        @block.vector
        def _(dve):
            n = [0]

            def link(ins):
                n[0] += 1
                ins.then_inc(sem("dve_chain"), 1)
                dve.wait_ge(sem("dve_chain"), n[0])

            dve.wait_ge(sem("par_mm"), 1)
            dve.tensor_copy(parT, PS[:, 4, 0:80]).then_inc(sem("par_ready"), 1)
            for c in range(KC):
                dve.wait_ge(sem("xT_mm"), c + 1)
                dve.tensor_copy(xT[:, c, :], PS[:, c % 4, 0:T]).then_inc(sem("xT_ready"), 1)
            dve.wait_ge(sem("dw_mm"), 1)
            link(dve.tensor_copy(dwT, PS[:, 5, 0:KC * KW].rearrange("p (c k) -> p c k", c=KC)))
            dve.wait_ge(sem("state_mm"), 1)
            dve.tensor_copy(uext[:, :, HALO + NP_:US], PS[:, 6, 0:KC * HALO].rearrange("p (c k) -> p c k", c=KC))\
               .then_inc(sem("state_ready"), 1)
            dve.wait_ge(sem("rb_in"), 16)
            dve.tensor_copy(rev_sb[:, 0:MAXREL - 1], rb_sb[:, NREL - 1:NREL].broadcast_to([H, MAXREL - 1]))
            dve.memset(rev_sb[:, REV - 1:REV], 0.0)
            dve.tensor_copy(rev_sb[:, MAXREL - 1:REV - 1], rb_sb[:, NREL - 1:0:-1]).then_inc(sem("rev_done"), 1)
            link(dve.memset(mv[:, :, :], 1.0))
            link(dve.memset(psumr[:, :], 1.0))
            dve.wait_ge(sem("uext_zero"), 1)
            for c in range(KC):
                dve.wait_ge(sem("proj_evac"), 4 + 8 + c + 1)
                dve.tensor_tensor(uext[:, c, HALO:HALO + NP_], ua[:, c, 0:NP_], ub[:, c, 0:NP_], ALU.mult).then_inc(sem("u_ready"), 1)
                dve.tensor_tensor(uext[:, c, US:US + NS_], ua[:, c, NP_:T], ub[:, c, NP_:T], ALU.mult).then_inc(sem("u_ready"), 1)
            dve.wait_ge(sem("u_ready"), 2 * KC)
            dve.wait_ge(sem("rev_out"), 16)
            for c in range(KC):
                dve.tensor_scalar(yc[:, c, :], uext[:, c, 0:CONVN], dwT[:, c, 0:1], parT[:, 56 + c:57 + c],
                                  ALU.mult, ALU.add).then_inc(sem("conv"), 1)
            with dve.Fori(1, KW) as k:
                for c in range(KC):
                    dve.wait_ge(sem("conv"), k * KC + (c + 1 - KC))
                    dve.scalar_tensor_tensor(
                        yc[:, c, :], uext[:, c, bass.ds(k, CONVN)],
                        dwT[:, c, bass.ds(k, 1)], yc[:, c, :], ALU.mult, ALU.add).then_inc(sem("conv"), 1)
            dve.wait_ge(sem("mean_mm"), 1)

            def over_chunks(ap, n):
                return ap.rearrange("p (a n) -> p a n", a=1).broadcast_to([P, KC, n])

            dve.tensor_tensor(zc[:, :, 0:NP_], yc[:, :, 0:NP_], over_chunks(PS[:, 4, 0:NP_], NP_),
                              ALU.subtract).then_inc(sem("zc_centred"), 1)
            dve.tensor_tensor(zc[:, :, NP_:T], yc[:, :, NP_ + HALO:CONVN], over_chunks(PS[:, 4, NP_ + HALO:CONVN], NS_),
                              ALU.subtract).then_inc(sem("zc_centred"), 1)
            dve.wait_ge(sem("bv_in"), 16)

            def values(s):
                for tt, (_, r) in enumerate(TT):
                    dve.wait_ge(sem("v_mm"), 3 * s + tt + 1)
                    dve.tensor_tensor(vtok[0:r, tt, 512 * s:512 * s + 512], PS[0:r, [0, 1, 2, 3, 6, 7][3 * s + tt], :],
                                      bv_bc[0:r, 512 * s:512 * s + 512], ALU.add).then_inc(sem("v_ready"), 1)

            values(0)
            dve.wait_ge(sem("std_c"), 1)
            link(dve.reciprocal(rstd_c, rstd_c))
            dve.tensor_tensor(zc, zc, over_chunks(rstd_c, T), ALU.mult).then_inc(sem("z_norm"), 1)
            values(1)

            def score(j):
                pr = probs[j % 2]
                k = 6 * (j % 2)
                dve.wait_ge(sem("score_mm"), j + 1)
                if j == 0:
                    dve.wait_ge(sem("relb_in"), 16)
                    link(dve.memset(relb[0:64, :, 192:256], NEG))
                for o, w, r, bank, b0 in [(0, 256, 128, 0, 0), (512, 128, 128, 1, 128), (768, 192, 64, 2, 0)]:
                    ins = dve.scalar_tensor_tensor(
                        pr[0:r, o:o + 2 * w].rearrange("p (h k) -> p h k", h=2),
                        PS[0:r, bank, 0:2 * w].rearrange("p (h k) -> p h k", h=2), SCALE,
                        relb[0:r, 2 * j:2 * j + 2, b0:b0 + w], ALU.mult, ALU.add)
                link(ins)
                for a, (o, w, r) in enumerate([(0, 256, 128), (512, 128, 128), (768, 192, 64)]):
                    ins = dve.tensor_reduce(nmax[0:r, k + 2 * a:k + 2 * a + 2],
                                            pr[0:r, o:o + 2 * w].rearrange("p (h k) -> p h k", h=2),
                                            AXX, ALU.max, negate=True)
                ins.then_inc(sem("scores_ready"), 1)

            def normalise(j):
                pr = probs[j % 2]
                k = 6 * (j % 2)
                dve.wait_ge(sem("exp_done"), j + 1)
                link(dve.reciprocal(rsum[:, k:k + 6], psumr[:, k:k + 6]))
                for a, (o, w, r) in enumerate([(0, 256, 128), (512, 128, 128), (768, 192, 64)]):
                    v = pr[0:r, o:o + 2 * w].rearrange("p (h k) -> p h k", h=2)
                    ins = dve.tensor_tensor(v, v, rsum[0:r, k + 2 * a:k + 2 * a + 2].rearrange("p (h a) -> p h a", a=1)
                                            .broadcast_to([r, 2, w]), ALU.mult)
                ins.then_inc(sem("probs_ready"), 1)

            score(0)
            for j in range(PAIRS):
                normalise(j)
                dve.wait_ge(sem("pw_mm"), j + 1)
                dve.tensor_tensor(mixT[:, j, :], PS[:, 6 + j % 2, 0:T], gb[:, j, :], ALU.mult).then_inc(sem("pw_evac"), 1)
                if j + 1 < PAIRS:
                    if j >= 1:
                        dve.wait_ge(sem("p_mm"), j)
                    score(j + 1)
            for t in range(KC):
                dve.wait_ge(sem("ao_mm"), t + 1)
                ins = dve.tensor_tensor(ga[:, t, :], PS[:, t % 4, 0:T], ga[:, t, :], ALU.mult)
                link(ins)
                dve.tensor_tensor(mixT[:, t, :], mixT[:, t, :], ga[:, t, :], ALU.add).then_inc(sem("mix_ready"), 1)
            dve.wait_ge(sem("xr_ready"), 3)
            for s in range(2):
                for tt, (_, r) in enumerate(TT):
                    dve.wait_ge(sem("out_mm"), 3 * s + tt + 1)
                    c = slice(512 * s, 512 * s + 512)
                    dve.tensor_tensor(xtok[0:r, tt, c], xtok[0:r, tt, c], PS[0:r, 3 * s + tt, :], ALU.add)\
                       .then_inc(sem("x1_pre"), 1)
                    dve.wait_ge(sem("x1_pre"), 3 * s + tt + 1)
                    link(dve.bn_stats(stats[0:r, tt, 6 * s:6 * s + 6], xtok[0:r, tt, c]))
                    if s == 1:
                        dve.bn_aggr(mv[0:r, tt, :], stats[0:r, tt, :]).then_inc(sem("var1"), 1)
                        dve.wait_ge(sem("std1"), tt + 1)
                        link(dve.reciprocal(rstd[0:r, tt:tt + 1], rstd[0:r, tt:tt + 1]))
                        dve.wait_ge(sem("ln1_in"), 32)
                        v = xtok[0:r, tt, :]
                        link(dve.tensor_scalar(v, v, mv[0:r, tt, 0:1], rstd[0:r, tt:tt + 1], ALU.subtract, ALU.mult))
                        link(dve.tensor_tensor(v, v, ln1g_bc[0:r], ALU.mult))
                        dve.tensor_tensor(v, v, ln1b_bc[0:r], ALU.add).then_inc(sem("x1_ready"), 1)
            dve.wait_ge(sem("k_out"), 32)
            link(dve.memset(chosen[:, 2, :], 0.0))
            link(dve.tensor_copy(tie, iota[0:E, 0:E]))
            link(dve.memset(tie[:, 0:1], -1e6))
            link(dve.memset(tie[:, 1:2], 1e6))
            dve.tensor_copy(above_at[:, 0:E:3], iota[0:E, 0:11])
            dve.tensor_scalar(above_at[:, 2:E:3], iota[0:E, 0:10], -2.0, float(E - 3), ALU.mult, ALU.add)
            link(dve.tensor_scalar(above_at[:, 1:E:3], iota[0:E, 0:11], -2.0, float(E - 2), ALU.mult, ALU.add))
            link(dve.memset(above_at[:, 1:2], float(E - 1)))
            link(dve.memset(above_at[:, E - 1:E], float(E - 2)))
            dve.wait_ge(sem("x1T_mm"), 2 * KC)
            dve.tensor_copy(yacc[:, :, NP_:T], PS[:, :, NP_:T]).then_inc(sem("x1T_d"), 1)
            for part in range(3):
                dve.memset(xh[64:128, part, 2, :], 0.0).then_inc(sem("xh_zero"), 1)
            dve.memset(scat[0], 0.0).then_inc(sem("scat_ready"), 1)
            dve.memset(scat[1], 0.0).then_inc(sem("scat_ready"), 1)
            dve.memset(ysb, 0.0).then_inc(sem("y_sb"), 1)
            dve.wait_ge(sem("wr_in"), 32)
            dve.wait_ge(sem("logit_mm"), 1)
            link(dve.tensor_tensor(lg, PS[:, 0, 384:384 + 3 * E].rearrange("p (t e) -> p t e", t=3),
                                   br_bc.rearrange("p (a e) -> p a e", a=1).broadcast_to([P, 3, E]), ALU.add))
            for tt in range(3):
                ins = dve.max(top8[:, tt, :], lg[:, tt, :])
            link(ins)
            dve.tensor_scalar(ntop, top8[:, :, 0], -1.0, None, ALU.mult).then_inc(sem("top_ready"), 1)
            for tt in range(3):
                ins = dve.max_index(idx8[:, tt, :], top8[:, tt, :], lg[:, tt, :])
            link(ins)
            link(dve.tensor_copy(idxf.rearrange("p (t k) -> p t k", t=3), idx8[:, :, 0:TOPK]))

            def by_expert(v):
                return v.rearrange("p (k a) -> p k a", a=1).broadcast_to([P, 3 * TOPK, E])

            terms = term.rearrange("p t k e -> p (t k) e")
            link(dve.tensor_tensor(terms, iota[:, 0:E].rearrange("p (a e) -> p a e", a=1).broadcast_to([P, 3 * TOPK, E]),
                                   by_expert(idxf), ALU.is_equal))
            dve.wait_ge(sem("e4_ready"), 3)
            link(dve.reciprocal(rs4, ssum))
            link(dve.tensor_tensor(e4, e4, rs4.rearrange("p (t a) -> p t a", a=1).broadcast_to([P, 3, TOPK]), ALU.mult))
            link(dve.tensor_tensor(terms, terms, by_expert(e4.rearrange("p t k -> p (t k)")), ALU.mult))
            link(dve.tensor_tensor(term[:, :, 0:2, :], term[:, :, 0:2, :], term[:, :, 2:4, :], ALU.add))
            link(dve.tensor_tensor(gates, term[:, :, 0, :], term[:, :, 1, :], ALU.add))
            dve.tensor_scalar(chosen[:, 0:2, :], gates[:, 0:2, :], 0.0, None, ALU.is_gt).then_inc(sem("chosen_ready"), 1)
            dve.tensor_scalar(chosen[0:NS_, 2, :], gates[0:NS_, 2, :], 0.0, None, ALU.is_gt).then_inc(sem("chosen_ready"), 1)
            dve.wait_ge(sem("rank_mm"), 1)
            dve.wait_ge(sem("chosen_ready"), 2)
            link(dve.tensor_tensor(rank, PS[:, 1, 0:3 * E].rearrange("p (t e) -> p t e", t=3), chosen, ALU.mult))
            link(dve.tensor_scalar(rank, rank, -1.0, None, ALU.add))
            total_row = PS[0:E, 1, 3 * E:4 * E]
            dve.scalar_tensor_tensor(key, total_row, 64.0, tie, ALU.mult, ALU.subtract)
            link(dve.tensor_tensor(diag[:, 1, :], total_row, ident[0:E, 0:E], ALU.mult))
            dve.tensor_tensor(diag[:, 2, :], iota[0:E, 0:E], ident[0:E, 0:E], ALU.mult)
            link(dve.tensor_tensor(diag[:, 0, :], key, ident[0:E, 0:E], ALU.mult))
            link(dve.tensor_reduce(cols, diag, AXX, ALU.add))
            link(dve.tensor_scalar(key, key, cols[:, 0:1], None, ALU.is_gt))
            link(dve.tensor_reduce(above, key, AXX, ALU.add))
            dve.tensor_scalar(at_place, above_at, above, None, ALU.is_equal).then_inc(sem("at_place_ready"), 1)
            dve.wait_ge(sem("order_mm"), 1)
            link(dve.tensor_copy(order, PS[0:1, 2, E:2 * E]))
            link(dve.tensor_copy(cnt, PS[0:1, 2, 0:E]))
            link(dve.tensor_scalar(nb, cnt, float(SLOTS), 1.0, ALU.is_gt, ALU.add))
            for b in range(2, T // SLOTS):
                link(dve.scalar_tensor_tensor(nb, cnt, float(SLOTS * b), nb, ALU.is_gt, ALU.add))
            link(dve.memset(one_r, 1.0))
            link(dve.tensor_tensor_scan(cum, one_r, nb, 0.0, ALU.mult, ALU.add))
            link(dve.memset(tbl[:, 0:1], 0))
            link(dve.tensor_copy(nblk, nb))
            link(dve.scalar_tensor_tensor(small, nb, -float(SLOTS), cnt, ALU.mult, ALU.add))
            link(dve.tensor_scalar(small, small, float(SMALL - SLOTS), None, ALU.is_le))
            link(dve.tensor_tensor(small, cum, small, ALU.subtract))
            link(dve.tensor_copy(tail, small))
            dve.tensor_copy(tbl[:, 1:E + 1], cum).then_inc(sem("tables_done"), 1)
            for c in range(KC):
                dve.wait_ge(sem("bias_mm"), c + 1)
                dve.scalar_tensor_tensor(yacc[:, c, :], yacc[:, c, :], ALPHA, PS[:, 4 + c % 4, 0:T], ALU.mult, ALU.add)\
                   .then_inc(sem("yacc"), 1)

            with dve.Fori(0, E) as e:
                first = dve.value_load(tbl[0:1, bass.ds(e, 1)], min_val=0, max_val=200)
                full = dve.value_load(tail[0:1, bass.ds(e, 1)], min_val=0, max_val=200)
                end = dve.value_load(tbl[0:1, bass.ds(e + 1, 1)], min_val=1, max_val=200)

                def expert_block(i, n):
                    dve.wait_ge(sem("gate_done"), i + 1)
                    dve.wait_ge(sem("hT_ready"), i + 1)
                    dve.tensor_scalar(gmin[:, 0:n], PS[:, 0, 0:n], LIMIT, None, ALU.min).then_inc(sem("gmin_ready"), 1)
                    dve.wait_ge(sem("sig_ready"), i + 1)
                    dve.tensor_tensor(act_h[:, 0:n], act_h[:, 0:n], gmin[:, 0:n], ALU.mult).then_inc(sem("gsig"), 1)
                    dve.wait_ge(sem("up_done"), i + 2)
                    dve.tensor_scalar(PS[:, 1, 0:n], PS[:, 1, 0:n], LIMIT, -LIMIT, ALU.min, ALU.max).then_inc(sem("upc"), 1)
                    dve.wait_ge(sem("gsig"), i + 1)
                    dve.wait_ge(sem("upc"), i + 1)
                    dve.scalar_tensor_tensor(act_h[:, 0:n], PS[:, 1, 0:n], 1.0, act_h[:, 0:n], ALU.add, ALU.mult).then_inc(sem("h_ready"), 1)
                    for c in range(KC):
                        dve.wait_ge(sem("comb_mm"), i * KC + (c + 1))
                        dve.tensor_tensor(yacc[:, c, :], yacc[:, c, :], PS[:, COMB_BANK[c], 0:T], ALU.add).then_inc(sem("yacc"), 1)
                    dve.wait_ge(sem("scat_mm"), i + 2)
                    w = 64 * n // 512
                    for r in range(0, P, w):
                        ins = dve.tensor_copy(scat[r // 64][r:r + w], PS[0:w, 4, 0:T])
                    ins.then_inc(sem("scat_ready"), 1)

                with dve.If(first < full):
                    with dve.Fori(first, full) as i:
                        expert_block(i, 512)
                with dve.If(full < end):
                    with dve.Fori(full, end) as i:
                        expert_block(i, 256)
            total = dve.value_load(tbl[0:1, E:E + 1], min_val=1, max_val=200)
            for c in range(KC):
                dve.wait_ge(sem("comb_mm"), total * KC + (c + 1))
                dve.tensor_tensor(yacc[:, c, :], yacc[:, c, :], PS[:, COMB_BANK[c], 0:T], ALU.add).then_inc(sem("yacc"), 1)
            for tt, (_, r) in enumerate(TT):
                for s in range(2):
                    dve.wait_ge(sem("y_mm"), 2 * tt + s + 1)
                    ins = dve.bn_stats(stats[0:r, tt, 6 * s:6 * s + 6], PS[0:r, 2 * tt + s, :])
            link(ins)
            for tt, (_, r) in enumerate(TT):
                ins = dve.bn_aggr(mv[0:r, tt, :], stats[0:r, tt, :])
            ins.then_inc(sem("var2"), 1)
            dve.wait_ge(sem("std2"), 1)
            link(dve.reciprocal(rstd, rstd))
            dve.scalar_tensor_tensor(nmax[:, 0:3], mv[:, :, 0], -1.0, rstd, ALU.mult, ALU.mult).then_inc(sem("shift2"), 1)
            dve.wait_ge(sem("ln2_in"), 32)
            for tt, (_, r) in enumerate(TT):
                v = WG[0][0:r, 2 + tt, :]
                dve.wait_ge(sem("norm2"), tt + 1)
                link(dve.tensor_tensor(v, v, WG[0][0:r, 0, :], ALU.mult))
                dve.tensor_tensor(v, v, WG[0][0:r, 1, :], ALU.add).then_inc(sem("y_ready"), 1)

        @block.tensor
        def _(pe):
            def tr(out, in_):
                k = in_.shape[0]
                return pe.transpose(out, in_, ident[0:k, 0:k])

            pe.wait_ge(sem("ident_ready"), 1)
            pe.wait_ge(sem("par_in"), 96)
            tr(PS[:, 4, 0:80], par_rows).then_inc(sem("par_mm"), 1)
            pe.wait_ge(sem("x_in"), 32)
            for c in range(KC):
                if c >= 4:
                    pe.wait_ge(sem("xT_ready"), c - 3)
                for t0, r in TT:
                    ins = tr(PS[:, c % 4, t0:t0 + r], xtok[0:r, t0 // P, P * c:P * c + P])
                ins.then_inc(sem("xT_mm"), 1)
            for c in range(KC):
                ins = tr(PS[:, 5, KW * c:KW * c + KW], dw_rows[:, P * c:P * c + P])
            ins.then_inc(sem("dw_mm"), 1)
            for c in range(KC):
                ins = tr(PS[:, 6, HALO * c:HALO * c + HALO], st_rows[:, P * c:P * c + P])
            ins.then_inc(sem("state_mm"), 1)
            pe.wait_ge(sem("xT_ready"), KC)

            def channels(s, wait_bank):
                for t in range(4):
                    wait_bank(t)
                    for c in range(KC):
                        ins = pe.matmul(PS[:, t, 0:T], ring[s][:, c, P * t:P * t + P], xT[:, c, :],
                                        start=(c == 0), stop=(c == KC - 1))
                    ins.then_inc(sem("proj_mm"), 1)

            def proj(i):
                for s in range(2):
                    pe.wait_ge(sem(f"ring{s}"), i * 16 + 16)
                    channels(s, lambda t: pe.wait_ge(sem("proj_evac"), i * 8 + (4 * s + t + 1)))

            with pe.Fori(0, 4) as i:
                proj(i)
            pe.wait_ge(sem("ck_in"), 16)
            for h in range(2):
                for c in range(4):
                    ins = tr(PS[:, 7 - 3 * h, P * c:P * c + P], ck_tok[:, P * (4 * h + c):P * (4 * h + c) + P])
                ins.then_inc(sem("ck_mm"), 1)
            pe.wait_ge(sem("u_ready"), 2 * KC)
            pe.wait_ge(sem("state_ready"), 1)
            pe.wait_ge(sem("ckT_ready"), 2)
            for b in range(4):
                col = (HALO + NP_ - HALO) if b < 2 else (US + NS_ - HALO)
                for c in range(4):
                    ins = tr(PS[0:HALO, 4 + b, P * c:P * c + P], uext[:, 4 * (b % 2) + c, col:col + HALO])
                ins.then_inc(sem("convout_mm"), 1)
            with pe.Fori(4, 6) as i:
                proj(i)
            pe.wait_ge(sem("consts"), 1)
            pe.wait_ge(sem("conv"), KW * KC)
            pe.wait_ge(sem("convout_ready"), 4)
            for c in range(KC):
                ins = pe.matmul(PS[:, 4, 0:CONVN], mean_w, yc[:, c, :], start=(c == 0), stop=(c == KC - 1))
            ins.then_inc(sem("mean_mm"), 1)

            def values(s):
                pe.wait_ge(sem(f"ring{s}"), 16 * 7)
                for tt, (t0, r) in enumerate(TT):
                    bank = [0, 1, 2, 3, 6, 7][3 * s + tt]
                    for c in range(KC):
                        ins = pe.matmul(PS[0:r, bank, :], xT[:, c, t0:t0 + r], ring[s][:, c, :],
                                        start=(c == 0), stop=(c == KC - 1))
                    ins.then_inc(sem("v_mm"), 1)

            pe.wait_ge(sem("proj_evac"), 4 + 48)
            values(0)
            pe.wait_ge(sem("sq_ready"), 1)
            for c in range(KC):
                ins = pe.matmul(PS[:, 5, 0:T], mean_w, sq[:, c, :], start=(c == 0), stop=(c == KC - 1))
            ins.then_inc(sem("var_mm"), 1)
            values(1)

            def scores(j):
                if j >= 1:
                    pe.wait_ge(sem("scores_ready"), j)
                else:
                    pe.wait_ge(sem("v_ready"), 6)
                for h in range(2):
                    q = qpad[h]
                    pe.matmul(PS[:, 0, 256 * h:256 * h + 256], q[:, j, P:2 * P], kT[:, j, 0:2 * P], start=True, stop=True)
                    pe.matmul(PS[:, 1, P * h:P * h + P], q[:, j, 0:P], kT[:, j, 0:P], start=True, stop=True)
                    pe.matmul(PS[0:NS_, 2, 192 * h:192 * h + P], q[:, j, 2 * P:T], ckT[:, j, :], start=True, stop=True)
                    ins = pe.matmul(PS[0:NS_, 2, 192 * h + P:192 * h + 192], q[:, j, 2 * P:T], kT[:, j, 2 * P:T],
                                    start=True, stop=True)
                ins.then_inc(sem("score_mm"), 1)

            def pointwise(j):
                s, t = j // 4, j % 4
                if t == 0:
                    pe.wait_ge(sem(f"ring{s}"), 16 * 8)
                if j >= 2:
                    pe.wait_ge(sem("pw_evac"), j - 1)
                for c in range(KC):
                    ins = pe.matmul(PS[:, 6 + j % 2, 0:T], ring[s][:, c, P * t:P * t + P], zc[:, c, :],
                                    start=(c == 0), stop=(c == KC - 1))
                ins.then_inc(sem("pw_mm"), 1)

            def transpose_probs(j):
                pr = probs[j % 2]
                pe.wait_ge(sem("probs_ready"), j + 1)
                if j >= 1:
                    pe.wait_ge(sem("pT_ready"), j)
                for h in range(2):
                    for kt in range(2):
                        tr(PS[:, 3, (2 * h + kt) * P:(2 * h + kt) * P + P], pr[:, 256 * h + P * kt:256 * h + P * kt + P])
                    tr(PS[:, 4, P * h:P * h + P], pr[:, 512 + P * h:512 + P * h + P])
                    tr(PS[:, 4, 256 + 64 * h:320 + 64 * h], pr[0:64, 768 + 192 * h:768 + 192 * h + P])
                    ins = tr(PS[0:64, 4, 384 + 64 * h:448 + 64 * h], pr[0:64, 768 + 192 * h + P:768 + 192 * h + 192])
                ins.then_inc(sem("p_mm"), 1)

            def attend(j):
                pt = pT[j % 2]
                pe.wait_ge(sem("pT_ready"), j + 1)
                if j >= 1:
                    pe.wait_ge(sem("o_ready"), j)
                for seg in range(3):
                    for h in range(2):
                        o = PS[64 * h:64 * h + 64, 5, :]
                        d = slice(HD * (2 * j + h), HD * (2 * j + h) + HD)
                        if seg == 0:
                            ins = pe.matmul(o[:, 0:P], vtok[:, 0, d], pt[:, 512 + P * h:512 + P * h + P], start=True, stop=True)
                        elif seg == 1:
                            for kt in range(2):
                                ins = pe.matmul(o[:, P:2 * P], vtok[:, kt, d], pt[:, (2 * h + kt) * P:(2 * h + kt) * P + P],
                                                start=(kt == 0), stop=(kt == 1))
                        else:
                            pe.matmul(o[:, 2 * P:T], cv_tok[:, d], pt[:, 768 + 64 * h:832 + 64 * h], start=True, stop=False)
                            ins = pe.matmul(o[:, 2 * P:T], vtok[0:64, 2, d], pt[0:64, 896 + 64 * h:960 + 64 * h],
                                            start=False, stop=True)
                ins.then_inc(sem("o_mm"), 1)

            pe.wait_ge(sem("z_ready"), KC)
            pe.wait_ge(sem("cv_in"), 16)
            scores(0)
            for j in range(PAIRS):
                pointwise(j)
                transpose_probs(j)
                if j + 1 < PAIRS:
                    scores(j + 1)
                attend(j)
            pe.wait_ge(sem("o_ready"), PAIRS)
            for t in range(KC):
                s = t // 4
                if t % 4 == 0:
                    pe.wait_ge(sem(f"ring{s}"), 16 * 9)
                if t >= 4:
                    pe.wait_ge(sem("mix_ready"), t - 3)
                for c in range(KC):
                    ins = pe.matmul(PS[:, t % 4, 0:T], ring[s][:, c, P * (t % 4):P * (t % 4) + P], oT[:, c, :],
                                    start=(c == 0), stop=(c == KC - 1))
                ins.then_inc(sem("ao_mm"), 1)
            pe.wait_ge(sem("pw_evac"), PAIRS)
            for b in range(6):
                tt, half = b // 2, b % 2
                t0, r = TT[tt]
                if b >= 4:
                    pe.wait_ge(sem("ktok_ready"), b - 3)
                for c in range(4):
                    ins = tr(PS[0:r, 4 + b % 4, P * c:P * c + P], kT[:, 4 * half + c, t0:t0 + r])
                ins.then_inc(sem("ktok_mm"), 1)
            pe.wait_ge(sem("mix_ready"), KC)
            for s in range(2):
                pe.wait_ge(sem(f"ring{s}"), 16 * 10)
                for tt, (t0, r) in enumerate(TT):
                    if s == 1 and tt == 1:
                        pe.wait_ge(sem("ktok_ready"), 6)
                    for c in range(KC):
                        ins = pe.matmul(PS[0:r, 3 * s + tt, :], mixT[:, c, t0:t0 + r], ring[s][:, c, :],
                                        start=(c == 0), stop=(c == KC - 1))
                    ins.then_inc(sem("out_mm"), 1)
            def transposed(tiles):
                for c in range(KC):
                    for t0, r in tiles:
                        ins = tr(PS[:, c, t0:t0 + r], xtok[0:r, t0 // P, P * c:P * c + P])
                    ins.then_inc(sem("x1T_mm"), 1)

            def logits(rows, tt, t0):
                for c in range(KC):
                    ins = pe.matmul(PS[rows, 0, 384 + E * tt:384 + E * tt + E], yacc[:, c, t0:t0 + rows.stop - rows.start],
                                    wr[:, c, :], start=(c == 0), stop=(c == KC - 1))
                return ins

            pe.wait_ge(sem("x1_pre"), 6)
            pe.wait_ge(sem("x1_ready"), 2)
            transposed(TT[:2])
            pe.wait_ge(sem("x1T_a"), KC)
            pe.wait_ge(sem("wr_in"), 32)
            for tt in range(2):
                logits(slice(0, P), tt, P * tt)
            pe.wait_ge(sem("x1_ready"), 3)
            transposed(TT[2:])
            pe.wait_ge(sem("x1T_d"), 1)
            logits(slice(0, NS_), 2, NP_)
            logits(slice(NS_, P), 2, NP_).then_inc(sem("logit_mm"), 1)
            pe.wait_ge(sem("tri_ready"), 2)
            pe.wait_ge(sem("chosen_ready"), 2)
            for tt in range(3):
                for s in range(tt + 1):
                    pe.matmul(PS[:, 1, E * tt:E * tt + E], tri if s == tt else ones16, chosen[:, s, :],
                              start=(s == 0), stop=(s == tt))
            for s in range(3):
                ins = pe.matmul(PS[:, 1, 3 * E:4 * E], ones16, chosen[:, s, :], start=(s == 0), stop=(s == 2))
            ins.then_inc(sem("rank_mm"), 1)
            for t0, r in TT:
                ins = tr(PS[0:E, 3, t0:t0 + r], gates[0:r, t0 // P, :])
            ins.then_inc(sem("gT_mm"), 1)
            pe.wait_ge(sem("at_place_ready"), 1)
            for k in range(2):
                ins = pe.matmul(PS[0:1, 2, E * k:E * k + E], cols[:, 1 + k:2 + k], at_place, start=True, stop=True)
            ins.then_inc(sem("order_mm"), 1)
            pe.wait_ge(sem("gT_ready"), 1)
            pe.wait_ge(sem("bdown_in"), 16)
            for c in range(KC):
                if c >= 4:
                    pe.wait_ge(sem("yacc"), c - 3)
                pe.matmul(PS[:, 4 + c % 4, 0:T], bdown_sb[:, P * c:P * c + P], gT, start=True, stop=True)\
                  .then_inc(sem("bias_mm"), 1)

            def gather(need):
                pe.wait_ge(sem("sel_ready"), need)
                for c in range(KC):
                    for tt in range(3):
                        for part in range(3):
                            ins = pe.matmul(PS[:, 2, SLOTS * c:SLOTS * c + SLOTS], xh[:, part, tt, P * c:P * c + P],
                                            sel[:, tt, :], start=(tt == 0 and part == 0), stop=(tt == 2 and part == 2))
                ins.then_inc(sem("gather_done"), 1)

            def gate_or_up(par, bank, w, which, half, done, parts):
                s, n = P // parts, D // parts
                for h in range(parts):
                    pe.matmul(PS[s * h:s * h + s, bank, 0:n], bsel[par][:, 0:s], bparts[:, which, n * h:n * h + n],
                              start=True, stop=False)
                for c in range(KC):
                    if c == 0:
                        pe.wait_ge(sem(w[1] + "_0"), w[2])
                    if c == 4:
                        pe.wait_ge(sem(w[1] + "_1"), w[2])
                    for h in range(parts):
                        ins = pe.matmul(PS[s * h:s * h + s, bank, 0:n], xg[:, c, 0:s], w[0][:, c, n * h:n * h + n],
                                        start=False, stop=(c == KC - 1))
                    if c == KC // 2 - 1:
                        ins.then_inc(sem(half), 1)
                ins.then_inc(sem(done), 1)

            def combine(base, chunks):
                for c in chunks:
                    if c < 2:
                        pe.wait_ge(sem("yacc"), base + (KC - 1 + c))
                    elif c > 2:
                        pe.wait_ge(sem("yacc"), base + (KC - 2 + c))
                    pe.matmul(PS[:, COMB_BANK[c], 0:T], ysb[:, P * (c % 4):P * (c % 4) + P], scat[c // 4],
                              start=True, stop=True).then_inc(sem("comb_mm"), 1)

            pe.wait_ge(sem("lo_ready"), 3)
            pe.wait_ge(sem("xh_zero"), 3)
            pe.wait_ge(sem("bparts_ready"), 2)
            gather(2)
            pe.wait_ge(sem("yacc"), KC)
            with pe.Fori(0, E // 2) as q:
                starts = [pe.value_load(tbl[0:1, bass.ds(q * 2 + k, 1)], min_val=0, max_val=200) for k in range(3)]
                tails = [pe.value_load(tail[0:1, bass.ds(q * 2 + k, 1)], min_val=0, max_val=200) for k in range(2)]
                for par in range(2):
                    e = q * 2 + par
                    first, full, end = starts[par], tails[par], starts[par + 1]

                    def expert_block(i, parts):
                        pe.wait_ge(sem("bsel_ready"), e + 1)
                        pe.wait_ge(sem("xg_ready"), i + 1)
                        gate_or_up(par, 0, (WG[par], f"wg{par}", q * 16 + 16), 0, "gate_half", "gate_done", parts)
                        pe.wait_ge(sem("yacc"), i * KC + (KC - 2))
                        gate_or_up(par, 1, (WU[par], f"wu{par}", q * 16 + 16), 1, "up_half", "up_done", parts)
                        gather(i + 3)
                        pe.wait_ge(sem("y_sb"), i + 1)
                        pe.wait_ge(sem("scat_ready"), i + 2)
                        combine(i * KC, range(2))
                        pe.wait_ge(sem("h_ready"), i + 1)
                        for c in range(KC // parts):
                            ins = tr(PS[:, 3, P * c:P * c + P], act_h[:, P * c:P * c + P])
                        ins.then_inc(sem("hT_mm"), 1)
                        combine(i * KC, range(2, KC))
                        apart(pe)
                        pe.wait_ge(sem("sgate_ready"), i + 2)
                        for t0, r in TT:
                            ins = tr(PS[0:P // parts, 4, t0:t0 + r], sgate[0:r, t0 // P, 0:P // parts])
                        ins.then_inc(sem("scat_mm"), 1)
                        pe.wait_ge(sem("hT_ready"), i + 2)
                        if parts == 2:
                            for c in range(KC):
                                if c % 4 == 0:
                                    pe.wait_ge(sem(f"wd_{c // 4}"), e * 16 + 16)
                                for h in range(2):
                                    ins = pe.matmul(PS[64 * h:64 * h + 64, 5, :], hT[:, c % 4, c // 4, :],
                                                    WD[:, c, 512 * h:512 * h + 512], start=(c == 0), stop=(c == KC - 1))
                                if c == KC // 2 - 1:
                                    ins.then_inc(sem("down_half"), 1)
                        else:
                            for c in range(4):
                                if c % 2 == 0:
                                    pe.wait_ge(sem(f"wd_{c // 2}"), e * 16 + 16)
                                for h in range(2):
                                    for k in range(2):
                                        r, ck = 64 * h + SMALL * k, 2 * c + k
                                        ins = pe.matmul(PS[r:r + SMALL, 5, :], hT_small[:, ck % 2, ck // 2, :],
                                                        WD[:, ck, 512 * h:512 * h + 512], start=(c == 0), stop=(c == 3))
                                if c == 1:
                                    ins.then_inc(sem("down_half"), 1)
                        ins.then_inc(sem("down_done"), 1)

                    with pe.If(first < full):
                        with pe.Fori(first, full) as i:
                            expert_block(i, 2)
                    with pe.If(full < end):
                        with pe.Fori(full, end) as i:
                            expert_block(i, 4)
            total = pe.value_load(tbl[0:1, E:E + 1], min_val=1, max_val=200)
            pe.wait_ge(sem("y_sb"), total + 1)
            pe.wait_ge(sem("scat_ready"), total + 2)
            combine(total * KC, range(KC))
            pe.wait_ge(sem("yacc"), total * KC + 2 * KC)
            for tt, (t0, r) in enumerate(TT):
                for s in range(2):
                    for c in range(4):
                        ins = tr(PS[0:r, 2 * tt + s, P * c:P * c + P], yacc[:, 4 * s + c, t0:t0 + r])
                    ins.then_inc(sem("y_mm"), 1)


_INS = ["x_prompt", "x_sample", "cache_k", "cache_v", "state_conv", "w_in", "b_in", "rel_bias", "w_att_o",
        "w_dw", "b_dw", "conv_ln_g", "conv_ln_b", "w_pw", "w_out", "b_out", "ln1_g", "ln1_b", "w_router",
        "b_router", "w_gate", "b_gate", "w_up", "b_up", "w_down", "b_down", "ln2_g", "ln2_b"]
_OUTS = [(1, 256, 1024), (1, 64, 1024), (1, 1, 256, 16, 64), (1, 1, 256, 16, 64), (1, 1, 30, 1024),
         (1, 1, 128, 16, 64), (1, 1, 128, 16, 64), (1, 1, 30, 1024)]


def kernel(**inputs):
    import numpy as _np
    import concourse.bacc as _bacc
    from concourse import mybir as _mybir
    from concourse.bass_utils import run_bass_kernel_spmd as _run

    nc = _bacc.Bacc("TRN2", target_bir_lowering=False, num_devices=1)
    arrays, args = {}, []
    for name in _INS:
        a = _np.ascontiguousarray(inputs[name])
        arrays[f"in_{name}_dram"] = a
        args.append(nc.dram_tensor(f"in_{name}_dram", a.shape, _mybir.dt.from_np(a.dtype), kind="ExternalInput").ap())
    for i, shape in enumerate(_OUTS):
        args.append(nc.dram_tensor(f"out_{i}_dram", shape, _mybir.dt.float32, kind="ExternalOutput").ap())
    encoder_step(nc, *args)
    r = _run(nc, [arrays], core_ids=[0])
    return tuple(r.results[0][f"out_{i}_dram"] for i in range(len(_OUTS)))
```
